# Optimizing a Trainium2 kernel written in Bass

```python
import functools
import jax, jax.numpy as jnp
from jax import lax
import numpy as np

D_MODEL = 2048
BATCH = 1
SEQ = 512
DEPTH = 1
DEC_BATCH = 8
DEC_SEQ = 16
PAST_LEN = 1024

CHUNK = 64
HEAD_DIM = 128
H_FOX = 8
H_BAND = 8
W_FOX = H_FOX * HEAD_DIM
W_BAND = H_BAND * HEAD_DIM
LEFT_CHUNKS = 8
BAND_CHUNKS = LEFT_CHUNKS + 1
BAND_WINDOW = LEFT_CHUNKS * CHUNK
REL_MAX = 128
Q_BLOCK = 128
N_KEYS = 128
N_EXPERTS = N_KEYS * N_KEYS
PEER_HEADS = 8
PEER_TOPK = 16
PEER_QDIM = 256
PEER_HALF = PEER_QDIM // 2
PEER_BLOCK = 128
EPS = 1e-6
FORGET_BIAS = 3.0
ADA_SCALE = 0.5
C_IN = 3 * W_FOX + H_FOX + 3 * W_BAND + 2 * D_MODEL

kernel_name = 'fox_band_peer_adaln_streaming_step'

def _rmsnorm(x, g):
    xf = x.astype(jnp.float32)
    y = xf * lax.rsqrt(jnp.mean(xf * xf, axis=-1, keepdims=True) + EPS)
    return (y * g.astype(jnp.float32)).astype(x.dtype)

def _adaln(c, w_ada, b_ada):
    h = jax.nn.silu(c) @ w_ada + b_ada
    return jnp.split(h[:, None, :], 6, axis=-1)

def _mixer_inputs(xm, w_in, b_forget):
    B, T, _ = xm.shape
    h = xm @ w_in
    sizes = (W_FOX, W_FOX, W_FOX, H_FOX, W_BAND, W_BAND, W_BAND, D_MODEL, D_MODEL)
    parts, o = [], 0
    for s in sizes:
        parts.append(h[..., o:o + s])
        o += s
    fq, fk, fv, ff, bq, bk, bv, ga, gb = parts
    hd = lambda t, n: t.reshape(B, T, n, HEAD_DIM)
    logf = jax.nn.log_sigmoid(ff.astype(jnp.float32) + b_forget.astype(jnp.float32))
    return (hd(fq, H_FOX), hd(fk, H_FOX), hd(fv, H_FOX), logf,
            hd(bq, H_BAND), hd(bk, H_BAND), hd(bv, H_BAND), ga, gb)

def _fox_attend(q, k, v, Fq, Fk, pos_q, pos_k):
    logits = jnp.einsum('bqhd,bkhd->bhqk', q, k).astype(jnp.float32) * (HEAD_DIM ** -0.5)
    decay = Fq[..., :, None] - Fk[..., None, :]
    logits = jnp.where(pos_k[None, :] <= pos_q[:, None], logits + decay, -jnp.inf)
    p = jax.nn.softmax(logits, axis=-1).astype(v.dtype)
    return jnp.einsum('bhqk,bkhd->bqhd', p, v)

def _fox_prompt(q, k, v, logf):
    B, S, H, _ = q.shape
    F = jnp.transpose(jnp.cumsum(logf, axis=1), (0, 2, 1))
    nb = S // Q_BLOCK
    qb = jnp.moveaxis(q.reshape(B, nb, Q_BLOCK, H, HEAD_DIM), 1, 0)
    Fb = jnp.moveaxis(F.reshape(B, H, nb, Q_BLOCK), 2, 0)
    pos_k = jnp.arange(S)

    def one_block(args):
        qi, Fi, i = args
        return _fox_attend(qi, k, v, Fi, F, i * Q_BLOCK + jnp.arange(Q_BLOCK), pos_k)

    y = lax.map(one_block, (qb, Fb, jnp.arange(nb)))
    y = jnp.moveaxis(y, 0, 1).reshape(B, S, H * HEAD_DIM)
    return y, (k, v, logf)

def _fox_sample(q, k, v, logf, cache_k, cache_v, cache_logf):
    B, T, H, _ = q.shape
    P = cache_k.shape[1]
    k_all = jnp.concatenate([cache_k.astype(k.dtype), k], axis=1)
    v_all = jnp.concatenate([cache_v.astype(v.dtype), v], axis=1)
    lf_all = jnp.concatenate([cache_logf.astype(jnp.float32), logf], axis=1)
    F = jnp.transpose(jnp.cumsum(lf_all, axis=1), (0, 2, 1))
    y = _fox_attend(q, k_all, v_all, F[..., P:], F, P + jnp.arange(T), jnp.arange(P + T))
    return y.reshape(B, T, H * HEAD_DIM), (k, v, logf)

def _rel_bias(d, rel_bias):
    return rel_bias[:, jnp.clip(d, -REL_MAX, REL_MAX) + REL_MAX].astype(jnp.float32)

def _band_prompt(q, k, v, rel_bias):
    B, S, H, _ = q.shape
    nc = S // CHUNK
    L = BAND_CHUNKS * CHUNK
    idx = jnp.arange(nc)[:, None] + jnp.arange(BAND_CHUNKS)[None, :]

    def band(t):
        tc = t.reshape(B, nc, CHUNK, H, HEAD_DIM)
        tc = jnp.pad(tc, ((0, 0), (LEFT_CHUNKS, 0), (0, 0), (0, 0), (0, 0)))
        return tc[:, idx].reshape(B, nc, L, H, HEAD_DIM)

    kb, vb = band(k), band(v)
    qc = q.reshape(B, nc, CHUNK, H, HEAD_DIM)
    logits = jnp.einsum('bnqhd,bnkhd->bhnqk', qc, kb).astype(jnp.float32) * (HEAD_DIM ** -0.5)
    d = BAND_WINDOW + jnp.arange(CHUNK)[:, None] - jnp.arange(L)[None, :]
    bias = _rel_bias(d, rel_bias)
    key_chunk = jnp.arange(nc)[:, None] - LEFT_CHUNKS + jnp.arange(BAND_CHUNKS)[None, :]
    valid = jnp.repeat(key_chunk >= 0, CHUNK, axis=1)
    logits = jnp.where(valid[None, None, :, None, :], logits + bias[None, :, None], -jnp.inf)
    p = jax.nn.softmax(logits, axis=-1).astype(vb.dtype)
    y = jnp.einsum('bhnqk,bnkhd->bnqhd', p, vb).reshape(B, S, H * HEAD_DIM)
    W = min(BAND_WINDOW, S)
    return y, (k[:, S - W:], v[:, S - W:])

def _band_sample(q, k, v, cache_k, cache_v, rel_bias):
    B, T, H, _ = q.shape
    W = cache_k.shape[1]
    k_all = jnp.concatenate([cache_k.astype(k.dtype), k], axis=1)
    v_all = jnp.concatenate([cache_v.astype(v.dtype), v], axis=1)
    d = W + jnp.arange(T)[:, None] - jnp.arange(W + T)[None, :]
    logits = jnp.einsum('bqhd,bkhd->bhqk', q, k_all).astype(jnp.float32) * (HEAD_DIM ** -0.5)
    logits = logits + _rel_bias(d, rel_bias)[None]
    p = jax.nn.softmax(logits, axis=-1).astype(v_all.dtype)
    y = jnp.einsum('bhqk,bkhd->bqhd', p, v_all)
    return y.reshape(B, T, H * HEAD_DIM), (k, v)

def _peer(x, w_query, sub_keys, expert_u, expert_v):
    B, T, D = x.shape
    n = B * T
    nb = -(-n // PEER_BLOCK)
    xt = jnp.pad(x.reshape(n, D), ((0, nb * PEER_BLOCK - n), (0, 0)))

    def one_block(xb):
        q = (xb @ w_query).reshape(PEER_BLOCK, PEER_HEADS, 2, PEER_HALF)
        s = jnp.einsum('thcd,hcnd->thcn', q, sub_keys).astype(jnp.float32)
        s1, i1 = lax.top_k(s[:, :, 0], PEER_TOPK)
        s2, i2 = lax.top_k(s[:, :, 1], PEER_TOPK)
        cand = (s1[..., :, None] + s2[..., None, :]).reshape(PEER_BLOCK, PEER_HEADS, PEER_TOPK * PEER_TOPK)
        top_s, top_c = lax.top_k(cand, PEER_TOPK)
        e = (jnp.take_along_axis(i1, top_c // PEER_TOPK, axis=-1) * N_KEYS
             + jnp.take_along_axis(i2, top_c % PEER_TOPK, axis=-1))
        g = jax.nn.softmax(top_s, axis=-1).astype(xb.dtype)
        h = jax.nn.gelu(jnp.einsum('thkd,td->thk', expert_u[e], xb), approximate=False)
        return jnp.einsum('thk,thkd->td', g * h, expert_v[e])

    y = lax.map(one_block, xt.reshape(nb, PEER_BLOCK, D))
    return y.reshape(nb * PEER_BLOCK, D)[:n].reshape(B, T, D)

def _block(x, c, fox_fn, band_fn, w_ada, b_ada, norm_mix, norm_ffn, w_in, b_forget,
           w_branch_fox, w_branch_band, w_out, w_query, sub_keys, expert_u, expert_v):
    sh1, sc1, g1, sh2, sc2, g2 = _adaln(c, w_ada, b_ada)
    xm = _rmsnorm(x, norm_mix) * (1 + sc1) + sh1
    fq, fk, fv, logf, bq, bk, bv, ga, gb = _mixer_inputs(xm, w_in, b_forget)
    ya, fox_state = fox_fn(fq, fk, fv, logf)
    yb, band_state = band_fn(bq, bk, bv)
    merged = jax.nn.sigmoid(ga) * (ya @ w_branch_fox) + jax.nn.sigmoid(gb) * (yb @ w_branch_band)
    x = x + g1 * (merged @ w_out)
    xf = _rmsnorm(x, norm_ffn) * (1 + sc2) + sh2
    x = x + g2 * _peer(xf, w_query, sub_keys, expert_u, expert_v)
    return x, fox_state + band_state

def setup_inputs(seed: int = 0) -> dict:
    key = jax.random.key(seed)
    ks = jax.random.split(key, 24)
    nrm = lambda k, shape, s: jax.random.normal(k, shape, jnp.float32) * s
    band_len = min(BAND_WINDOW, PAST_LEN)
    return {
        'x_prompt': nrm(ks[0], (BATCH, SEQ, D_MODEL), 1.0),
        'x_sample': nrm(ks[1], (DEC_BATCH, DEC_SEQ, D_MODEL), 1.0),
        'c_prompt': nrm(ks[2], (BATCH, D_MODEL), 1.0),
        'c_sample': nrm(ks[3], (DEC_BATCH, D_MODEL), 1.0),
        'cache_fox_k': nrm(ks[4], (DEPTH, DEC_BATCH, PAST_LEN, H_FOX, HEAD_DIM), 1.0),
        'cache_fox_v': nrm(ks[5], (DEPTH, DEC_BATCH, PAST_LEN, H_FOX, HEAD_DIM), 1.0),
        'cache_fox_logf': jax.nn.log_sigmoid(FORGET_BIAS + nrm(ks[6], (DEPTH, DEC_BATCH, PAST_LEN, H_FOX), 1.0)),
        'cache_band_k': nrm(ks[7], (DEPTH, DEC_BATCH, band_len, H_BAND, HEAD_DIM), 1.0),
        'cache_band_v': nrm(ks[8], (DEPTH, DEC_BATCH, band_len, H_BAND, HEAD_DIM), 1.0),
        'w_ada': nrm(ks[9], (DEPTH, D_MODEL, 6 * D_MODEL), ADA_SCALE * D_MODEL ** -0.5),
        'b_ada': nrm(ks[10], (DEPTH, 6 * D_MODEL), 0.01),
        'norm_mix': 1.0 + nrm(ks[11], (DEPTH, D_MODEL), 0.01),
        'norm_ffn': 1.0 + nrm(ks[12], (DEPTH, D_MODEL), 0.01),
        'w_in': nrm(ks[13], (DEPTH, D_MODEL, C_IN), D_MODEL ** -0.5),
        'b_forget': FORGET_BIAS + nrm(ks[14], (DEPTH, H_FOX), 0.5),
        'rel_bias': nrm(ks[15], (DEPTH, H_BAND, 2 * REL_MAX + 1), 0.5),
        'w_branch_fox': nrm(ks[16], (DEPTH, W_FOX, D_MODEL), W_FOX ** -0.5),
        'w_branch_band': nrm(ks[17], (DEPTH, W_BAND, D_MODEL), W_BAND ** -0.5),
        'w_out': nrm(ks[18], (DEPTH, D_MODEL, D_MODEL), D_MODEL ** -0.5),
        'w_query': nrm(ks[19], (DEPTH, D_MODEL, PEER_HEADS * PEER_QDIM), D_MODEL ** -0.5),
        'sub_keys': nrm(ks[20], (DEPTH, PEER_HEADS, 2, N_KEYS, PEER_HALF), PEER_HALF ** -0.5),
        'expert_u': nrm(ks[21], (DEPTH, N_EXPERTS, D_MODEL), D_MODEL ** -0.5),
        'expert_v': nrm(ks[22], (DEPTH, N_EXPERTS, D_MODEL), 1.0),
        'norm_final': 1.0 + nrm(ks[23], (D_MODEL,), 0.01),
    }

def reference(x_prompt, x_sample, c_prompt, c_sample, cache_fox_k, cache_fox_v, cache_fox_logf,
              cache_band_k, cache_band_v, w_ada, b_ada, norm_mix, norm_ffn, w_in, b_forget, rel_bias,
              w_branch_fox, w_branch_band, w_out, w_query, sub_keys, expert_u, expert_v, norm_final):
    xp, xs = x_prompt, x_sample
    st_p, st_s = [], []
    for l in range(DEPTH):
        lw = (w_ada[l], b_ada[l], norm_mix[l], norm_ffn[l], w_in[l], b_forget[l], w_branch_fox[l],
              w_branch_band[l], w_out[l], w_query[l], sub_keys[l], expert_u[l], expert_v[l])
        band_p = functools.partial(_band_prompt, rel_bias=rel_bias[l])
        xp, sp = _block(xp, c_prompt, _fox_prompt, band_p, *lw)
        fox_s = functools.partial(_fox_sample, cache_k=cache_fox_k[l], cache_v=cache_fox_v[l],
                                  cache_logf=cache_fox_logf[l])
        band_s = functools.partial(_band_sample, cache_k=cache_band_k[l], cache_v=cache_band_v[l],
                                   rel_bias=rel_bias[l])
        xs, ss = _block(xs, c_sample, fox_s, band_s, *lw)
        st_p.append(sp)
        st_s.append(ss)
    fox_k_p, fox_v_p, fox_logf_p, band_k_p, band_v_p = [jnp.stack([s[i] for s in st_p]) for i in range(5)]
    fox_k_s, fox_v_s, fox_logf_s, band_k_s, band_v_s = [jnp.stack([s[i] for s in st_s]) for i in range(5)]
    y_prompt = _rmsnorm(xp, norm_final)
    y_sample = _rmsnorm(xs, norm_final)
    return (y_prompt, y_sample, fox_k_p, fox_v_p, fox_logf_p, band_k_p, band_v_p,
            fox_k_s, fox_v_s, fox_logf_s, band_k_s, band_v_s)


_drawn_inputs = setup_inputs


def setup_inputs(seed=0):
    import zlib

    import numpy as np

    out = dict(_drawn_inputs(seed))
    spreads = {}
    factors = {'cache_fox_logf': 13.344,
     'cache_band_k': 2.686,
     'norm_mix': 5.972,
     'norm_ffn': 11.108,
     'rel_bias': 2.801,
     'norm_final': 33.128}
    for name, (base, spread) in spreads.items():
        noise = np.random.default_rng([zlib.crc32(name.encode()), seed]).standard_normal(out[name].shape)
        drawn = base * np.exp(spread * noise) if base else spread * noise
        out[name] = __import__('jax').numpy.asarray(drawn.astype(out[name].dtype))
    for name, factor in factors.items():
        out[name] = (out[name] * factor).astype(out[name].dtype)
    return out
```

```python
from contextlib import ExitStack

import numpy as np

import concourse.bass as bass
from concourse import mybir

F32 = mybir.dt.float32
F32R = mybir.dt.float32r
U32 = mybir.dt.uint32
ALU = mybir.AluOpType
ACT = mybir.ActivationFunctionType
AX = mybir.AxisListType

P = 128
D = 2048
DC = D // P
TP = 512
NB, TS = 8, 16
T = TP + NB * TS
TT = T // P
HALF = T // 2
KT = 8
NC9 = 1 + NB
QUAD = 32
H = 8
HD = 128
PAST = 1024
BW = 512
REL = 128
NREL = 2 * REL + 1
RPAD = 400
QK_SCALE = HD ** -0.5
EPS = 1e-6
NEG = -1e30
LOWEST = -3e38
NKEY = 128
TOPK = 16
GROUP = 8
NGROUP = NKEY // GROUP
GB = 32
NGB = T // GB
RAW, SPLIT = 4, 2


class Chip:

    def __init__(self, nc, ctx):
        self.nc = nc
        self.ctx = ctx
        self.phase_sems = []
        self.passed = nc.alloc_semaphore(name="passed")
        self.act_hi = self.sb("act_hi", [P, DC, T], F32R)
        self.act_lo = self.sb("act_lo", [P, DC, T], F32R)
        self.acc = self.sb("acc", [P, DC, T], F32)
        self.ada = self.sb("ada", [P, 6 * DC, NC9], F32)
        self.ones = self.sb("ones", [P, P], F32)
        self.ident = self.sb("ident", [P, P], F32)
        self.flip = self.sb("flip", [P, P], F32)
        self.causal = self.sb("causal", [P, P], F32)
        self.head_rows = self.sb("head_rows", [H, H, TS], F32)
        self.query_rows = self.sb("query_rows", [TS, H, TS], F32)
        self.iota = self.sb("iota", [P, P], F32)
        self.scores = ctx.enter_context(nc.psum_tensor("scores", [P, 3 * 512], F32))
        rest = ctx.enter_context(nc.psum_tensor("rest", [P, 5 * 512], F32))
        self.bank = [self.scores[:, b * 512:(b + 1) * 512] for b in range(3)]
        self.bank += [rest[:, b * 512:(b + 1) * 512] for b in range(5)]

    def sb(self, name, shape, dt, ctx=None):
        return (ctx or self.ctx).enter_context(self.nc.sbuf_tensor(name, shape, dt))

    def sem(self, name):
        handle = self.nc.alloc_semaphore(name=name)
        self.phase_sems.append(handle)
        return handle

    def end_phase(self):
        self.nc.clear_and_free_semaphores(self.phase_sems)
        self.nc.all_engine_barrier()
        self.phase_sems = []

    def halves(self, b):
        return self.bank[b][:, 0:HALF], self.bank[b + 1][:, 0:HALF]


def own_instruction(c, eng):
    eng.sem_inc(c.passed, 1)


def first_then_loop(eng, count, step):
    step(0, True)
    with eng.Fori(1, count) as i:
        step(i, False)


def build_constants(c):
    nc = c.nc
    filled, done = c.sem("const_filled"), c.sem("const_done")
    with nc.Block() as block:
        @block.gpsimd
        def _(pool):
            pool.memset(c.ones[:], 1.0)
            pool.iota(c.iota[:], pattern=[[1, P]], base=0, channel_multiplier=0,
                      allow_small_or_imprecise_dtypes=True)
            pool.memset(c.ident[:], 0.0).then_inc(filled, 1)
            pool.memset(c.flip[:], 0.0).then_inc(filled, 1)
            pool.memset(c.causal[:], 0.0).then_inc(filled, 1)
            pool.memset(c.head_rows[:], 0.0).then_inc(filled, 1)
            pool.memset(c.query_rows[:], 0.0).then_inc(filled, 1)
            pool.wait_ge(filled, 5)
            pool.affine_select(out=c.ident[:], in_=c.ident[:], compare_op=ALU.not_equal, fill=1.0,
                               base=0, pattern=[[-1, P]], channel_multiplier=1)
            pool.affine_select(out=c.flip[:], in_=c.flip[:], compare_op=ALU.not_equal, fill=1.0,
                               base=1 - P, pattern=[[1, P]], channel_multiplier=1)
            pool.affine_select(out=c.causal[:], in_=c.causal[:], compare_op=ALU.is_ge, fill=NEG,
                               base=0, pattern=[[-1, P]], channel_multiplier=1)
            pool.affine_select(out=c.head_rows[:], in_=c.head_rows[:], compare_op=ALU.not_equal,
                               fill=1.0, base=0, pattern=[[1, H], [0, TS]], channel_multiplier=-1)
            pool.affine_select(out=c.query_rows[:], in_=c.query_rows[:], compare_op=ALU.not_equal,
                               fill=1.0, base=0, pattern=[[0, H], [1, TS]],
                               channel_multiplier=-1).then_inc(done, 1)
            pool.wait_ge(done, 1)


def build_ada(c, w_ada, b_ada, cond):
    nc = c.nc
    NW = 6 * D // 512
    KQ = DC // RAW
    FB = 512 // P
    with ExitStack() as tmp:
        ring = c.sb("ada_ring", [P, 2 * RAW, KQ, 512], F32, tmp)
        bias = c.sb("ada_bias", [P, 6 * DC], F32, tmp)
        cond_in = c.sb("cond_in", [P, DC, QUAD], F32, tmp)
        cond_act = c.sb("cond_act", [P, DC, QUAD], F32, tmp)
        rows = [c.sb(f"ada_rows{b}", [P, 512], F32, tmp) for b in range(2)]
        add_up = c.sb("ada_add_up", [P, NC9], F32, tmp)
        loaded = [c.sem(f"ada_loaded{s}") for s in range(2 * RAW)]
        small_in, cond_ready = c.sem("ada_small_in"), c.sem("ada_cond_ready")
        add_up_ready = c.sem("ada_add_up_ready")
        tile_used, product, rows_ready = c.sem("ada_tile_used"), c.sem("ada_product"), c.sem("ada_rows_ready")
        turned, read_out = c.sem("ada_turned"), c.sem("ada_read_out")
        with nc.Block() as block:
            @block.sync
            def _(sp):
                sp.dma_start(cond_in[:], cond).then_inc(small_in, 16)
                sp.dma_start(bias[:], b_ada).then_inc(small_in, 16)

                def load(i, first):
                    for s in range(2 * RAW):
                        if not first:
                            sp.wait_ge(tile_used, i * (2 * RAW) + (s + 1 - 2 * RAW))
                        sp.dma_start(ring[:, s], w_ada[i * (2 * RAW) + s]).then_inc(loaded[s], 16)

                first_then_loop(sp, NW * RAW // (2 * RAW), load)

            @block.scalar
            def _(act):
                act.wait_ge(small_in, 32)
                act.activation(cond_act[:], cond_in[:], ACT.Silu).then_inc(cond_ready, 1)

            @block.tensor
            def _(pe):
                def turn(n, b):
                    pe.wait_ge(rows_ready, n + 1)
                    for f in range(FB):
                        mm = pe.matmul(c.bank[2 + b][:, f * NC9:(f + 1) * NC9], rows[b][:, f * P:(f + 1) * P], add_up[:],
                                       start=True, stop=True)
                    mm.then_inc(turned, 1)

                def blocks(i, first):
                    for b in range(2):
                        n = i * 2 + b
                        if not first:
                            pe.wait_ge(rows_ready, n - 1)
                        for s in range(RAW):
                            pe.wait_ge(loaded[b * RAW + s], i * 16 + 16)
                            for k in range(KQ):
                                mm = pe.matmul(c.bank[b][k * QUAD:(k + 1) * QUAD, :], cond_act[:, s * KQ + k, :],
                                               ring[:, b * RAW + s, k, :], start=(s == 0), stop=(s == RAW - 1),
                                               skip_group_check=True)
                            mm.then_inc(tile_used, 1)
                        if not (first and b == 0):
                            if not (first and b == 1):
                                pe.wait_ge(read_out, n - 2)
                            turn(n - 1, (b + 1) % 2)

                pe.wait_ge(cond_ready, 1)
                pe.wait_ge(add_up_ready, 1)
                first_then_loop(pe, NW // 2, blocks)
                turn(NW - 1, 1)

            @block.vector
            def _(dve):
                def evacuate(i, first):
                    for b in range(2):
                        n = i * 2 + b
                        dve.wait_ge(tile_used, n * RAW + RAW)
                        if not first:
                            dve.wait_ge(turned, n - 1)
                        dve.tensor_copy(rows[b][:], c.bank[b][:]).then_inc(rows_ready, 1)
                        if not (first and b == 0):
                            finish(n - 1, (b + 1) % 2)

                def finish(n, b):
                    dve.wait_ge(turned, n + 1)
                    dve.tensor_tensor(c.ada[:, bass.ds(n * FB, FB), :],
                                      c.bank[2 + b][:, 0:FB * NC9].rearrange("p (f c) -> p f c", c=NC9),
                                      bias[:, bass.ds(n * FB, FB)].unsqueeze(2).broadcast_to([P, FB, NC9]),
                                      ALU.add).then_inc(read_out, 1)

                dve.tensor_reduce(add_up[:], c.ident[:].rearrange("p (g c) -> p c g", c=QUAD)[:, 0:NC9, :], AX.X,
                                  ALU.add).then_inc(add_up_ready, 1)
                dve.wait_ge(small_in, 32)
                first_then_loop(dve, NW // 2, evacuate)
                finish(NW - 1, 1)


def build_norm(c, name, x_dram, gain, scale_row, shift_row, out_dram=None):
    nc = c.nc
    NST = 4
    with ExitStack() as tmp:
        gains = c.sb(f"{name}_gains", [P, DC], F32, tmp)
        square = c.sb(f"{name}_square", [P, 2, T], F32, tmp)
        rstd = c.sb(f"{name}_rstd", [P, T], F32, tmp)
        normed = c.sb(f"{name}_normed", [P, 2, T], F32, tmp)
        value = c.sb(f"{name}_value", [P, 2 if out_dram is None else NST, T], F32, tmp)
        mult = c.sb(f"{name}_mult", [P, DC, NC9], F32, tmp)
        sem = {n: c.sem(f"{name}_{n}") for n in
               ("gain_in", "squared", "summed", "sum_done", "var", "root", "rstd_ready", "mult_ready",
                "normed", "affine", "sample_a", "sample", "hi", "lo", "out_used")}
        x_in = [c.sem(f"{name}_x_in{q}") for q in range(4)]
        stored = [c.sem(f"{name}_stored{b}") for b in range(NST)]
        sums = c.halves(0)
        with nc.Block() as block:
            @block.sync
            def _(sp):
                sp.dma_start(gains[:], gain).then_inc(sem["gain_in"], 16)
                if x_dram is not None:
                    for q in range(4):
                        sp.dma_start(c.acc[:, 4 * q:4 * q + 4, :],
                                     x_dram[4 * q:4 * q + 4].rearrange("k p t -> p k t")).then_inc(x_in[q], 16)
                if out_dram is not None:
                    with sp.Fori(0, DC // NST) as i:
                        for b in range(NST):
                            sp.wait_ge(sem["normed"], i * NST + (b + 1))
                            sp.dma_start(out_dram[i * NST + b], value[:, b, :]).then_inc(stored[b], 16)
                    for b in range(NST):
                        sp.wait_ge(stored[b], 16 * (DC // NST))

            @block.scalar
            def _(act):
                for k in range(DC):
                    if x_dram is not None and k % 4 == 0:
                        act.wait_ge(x_in[k // 4], 16)
                    if k >= 2:
                        act.wait_ge(sem["summed"], k - 1)
                    act.activation(square[:, k % 2, :], c.acc[:, k, :], ACT.Square).then_inc(sem["squared"], 1)
                act.wait_ge(sem["var"], 2)
                act.activation(rstd[:], rstd[:], ACT.Sqrt).then_inc(sem["root"], 1)
                if out_dram is None:
                    act.wait_ge(sem["mult_ready"], 1)
                    with act.Fori(0, DC // 2) as i:
                        for b in range(2):
                            k = i * 2 + b
                            act.wait_ge(sem["normed"], k + 1)
                            act.wait_ge(sem["lo"], k + 1)
                            act.activation(value[:, b, 0:TP], normed[:, b, 0:TP], ACT.Identity,
                                           scale=mult[:, k, 0:1],
                                           bias=c.ada[:, k + shift_row * DC, 0:1]).then_inc(sem["affine"], 1)
                            act.wait_ge(sem["affine"], k + 1)
                            act.wait_ge(sem["sample"], k + 1)
                            act.activation(c.act_hi[:, k, :], value[:, b, :], ACT.Copy).then_inc(sem["hi"], 1)

            @block.tensor
            def _(pe):
                for k in range(DC):
                    pe.wait_ge(sem["squared"], k + 1)
                    for h in range(2):
                        mm = pe.matmul(sums[h], c.ones[:], square[:, k % 2, h * HALF:(h + 1) * HALF],
                                       start=(k == 0), stop=(k == DC - 1))
                    mm.then_inc(sem["summed"], 1)

            @block.vector
            def _(dve):
                dve.wait_ge(sem["gain_in"], 16)
                if out_dram is None:
                    dve.scalar_tensor_tensor(out=mult[:], in0=c.ada[:, scale_row * DC:(scale_row + 1) * DC, :],
                                             scalar=1.0,
                                             in1=gains[:].unsqueeze(2).broadcast_to([P, DC, NC9]),
                                             op0=ALU.add, op1=ALU.mult).then_inc(sem["mult_ready"], 1)
                dve.wait_ge(sem["summed"], DC)
                for h in range(2):
                    dve.tensor_scalar(rstd[:, h * HALF:(h + 1) * HALF], sums[h], 1.0 / D, EPS,
                                      ALU.mult, ALU.add).then_inc(sem["var"], 1)
                dve.wait_ge(sem["root"], 1)
                dve.reciprocal(rstd[:], rstd[:]).then_inc(sem["rstd_ready"], 1)
                dve.wait_ge(sem["rstd_ready"], 1)
                if out_dram is not None:
                    for k in range(DC):
                        if k >= NST:
                            dve.wait_ge(stored[k % NST], 16 * (k // NST))
                        dve.scalar_tensor_tensor(out=value[:, k % NST, :], in0=c.acc[:, k, :],
                                                 scalar=gains[:, k:k + 1], in1=rstd[:],
                                                 op0=ALU.mult, op1=ALU.mult).then_inc(sem["normed"], 1)
                    return
                dve.wait_ge(sem["mult_ready"], 1)
                dve.sem_inc(sem["lo"], 2)

                def modulate(i, first):
                    for b in range(2):
                        k = i * 2 + b
                        row = normed[:, b, TP:T].rearrange("p (s t) -> p s t", s=NB)
                        val = value[:, b, TP:T].rearrange("p (s t) -> p s t", s=NB)
                        dve.wait_ge(sem["lo"], k + 1)
                        dve.tensor_tensor(normed[:, b, :], c.acc[:, k, :], rstd[:], ALU.mult).then_inc(sem["normed"], 1)
                        dve.wait_ge(sem["normed"], k + 1)
                        dve.tensor_tensor(val, row, mult[:, k, 1:NC9].unsqueeze(2).broadcast_to([P, NB, TS]),
                                          ALU.mult).then_inc(sem["sample_a"], 1)
                        dve.wait_ge(sem["sample_a"], k + 1)
                        dve.tensor_tensor(val, val, c.ada[:, k + shift_row * DC, 1:NC9].unsqueeze(2).broadcast_to([P, NB, TS]),
                                          ALU.add).then_inc(sem["sample"], 1)
                        if not (first and b == 0):
                            rest_of(k - 1, 1 - b)

                def rest_of(k, b):
                    dve.wait_ge(sem["hi"], k + 1)
                    dve.tensor_tensor(c.act_lo[:, k, :], value[:, b, :], c.act_hi[:, k, :].bitcast(F32),
                                      ALU.subtract).then_inc(sem["lo"], 1)

                first_then_loop(dve, DC // 2, modulate)
                rest_of(DC - 1, 1)


class WeightStream:

    def __init__(self, c, tmp, name):
        self.c = c
        self.raw = c.sb(f"{name}_raw", [P, RAW, KT * P], F32, tmp)
        self.hi = [c.sb(f"{name}_w_hi{s}", [P, KT * P], F32R, tmp) for s in range(SPLIT)]
        self.lo = [c.sb(f"{name}_w_lo{s}", [P, KT * P], F32R, tmp) for s in range(SPLIT)]
        self.loaded = [c.sem(f"{name}_loaded{s}") for s in range(RAW)]
        self.rounded = c.sem(f"{name}_rounded")
        self.split = c.sem(f"{name}_split")
        self.used = c.sem(f"{name}_used")

    def load_four(self, sp, tiles, n):
        for s in range(RAW):
            sp.wait_ge(self.split, n + (s + 1))
            sp.dma_start(self.raw[:, s], tiles[n + s]).then_inc(self.loaded[s], 16)

    def load(self, sp, tiles, count):
        with sp.Fori(0, count // RAW) as i:
            self.load_four(sp, tiles, i * RAW)

    def divide(self, pool, count):
        pool.sem_inc(self.split, RAW)
        pool.sem_inc(self.used, SPLIT)
        with pool.Fori(0, count // RAW) as i:
            for s in range(RAW):
                n = i * RAW + s
                pool.wait_ge(self.loaded[s], i * 16 + 16)
                pool.wait_ge(self.used, n + 1)
                own_instruction(self.c, pool)
                pool.tensor_tensor(self.hi[s % SPLIT][:].rearrange("p (k n) -> p k n", k=KT),
                                   self.raw[:, s].rearrange("p (k n) -> p k n", k=KT),
                                   self.c.ones[:, 0:1].unsqueeze(2).broadcast_to([P, KT, P]),
                                   ALU.mult).then_inc(self.rounded, 1)
                pool.wait_ge(self.rounded, n + 1)
                pool.tensor_tensor(self.lo[s % SPLIT][:], self.raw[:, s],
                                   self.hi[s % SPLIT][:].bitcast(F32), ALU.subtract).then_inc(self.split, 1)

    def multiply(self, pe, n, slot, out, x_hi, x_lo, k0, start, stop, chunk_ready=None, ready_from=0):
        pe.wait_ge(self.split, n + (1 + RAW))
        for k in range(KT):
            if chunk_ready is not None:
                pe.wait_ge(chunk_ready, ready_from + (k0 + k + 1))
            hi, lo = (w[slot][:, k * P:(k + 1) * P] for w in (self.hi, self.lo))
            for j, (w, x) in enumerate(((hi, x_hi), (hi, x_lo), (lo, x_hi))):
                for h in range(2):
                    mm = pe.matmul(out[h], w, x[:, k0 + k, h * HALF:(h + 1) * HALF],
                                   start=(start and k == 0 and j == 0), stop=(stop and k == KT - 1 and j == 2))
        mm.then_inc(self.used, 1)


def build_projection(c, w_heads, w_forget, b_forget, proj, logf):
    nc = c.nc
    NM = 6 * H
    with ExitStack() as tmp:
        ws = WeightStream(c, tmp, "proj")
        stage = c.sb("proj_stage", [P, 2, T], F32, tmp)
        fw = c.sb("forget_w", [P, DC, H], F32, tmp)
        fw_hi = c.sb("forget_w_hi", [P, DC, H], F32R, tmp)
        fw_lo = c.sb("forget_w_lo", [P, DC, H], F32R, tmp)
        fb = c.sb("forget_b", [P, H], F32, tmp)
        z, e, lg, mn = (c.sb(f"forget_{n}", [P, TT, H], F32, tmp) for n in ("z", "e", "log", "min"))
        small_in, fw_round, fw_ready = c.sem("proj_small_in"), c.sem("fw_round"), c.sem("fw_ready")
        half0, half1 = c.sem("proj_half0"), c.sem("proj_half1")
        stored = [c.sem(f"proj_stored{b}") for b in range(2)]
        forget, fstep, fact, fstored = c.sem("forget_product"), c.sem("forget_step"), c.sem("forget_act"), c.sem("forget_stored")
        out = [c.halves(0), c.halves(2)]
        with nc.Block() as block:
            @block.sync
            def _(sp):
                sp.dma_start(fw[:], w_forget).then_inc(small_in, 16)
                sp.dma_start(fb[:], b_forget).then_inc(small_in, 16)
                ws.load(sp, w_heads, 2 * NM)
                sp.wait_ge(fstep, 5)
                sp.dma_start(logf.rearrange("(t p) h -> p t h", p=P), lg[:]).then_inc(fstored, 16)
                sp.wait_ge(fstored, 16)

            @block.gpsimd
            def _(pool):
                ws.divide(pool, 2 * NM)

            @block.tensor
            def _(pe):
                pe.wait_ge(fw_ready, 1)
                for t in range(TT):
                    for k in range(DC):
                        xh, xl = (x[:, k, t * P:(t + 1) * P] for x in (c.act_hi, c.act_lo))
                        for j, (x, w) in enumerate(((xh, fw_hi), (xh, fw_lo), (xl, fw_hi))):
                            mm = pe.matmul(c.bank[4][:, t * H:(t + 1) * H], x, w[:, k, :],
                                           start=(k == 0 and j == 0), stop=(k == DC - 1 and j == 2))
                mm.then_inc(forget, 1)
                with pe.Fori(0, NM // 2) as i:
                    for b in range(2):
                        m = i * 2 + b
                        pe.wait_ge(half0, m + 1)
                        pe.wait_ge(half1, m + 1)
                        for kh in range(2):
                            ws.multiply(pe, m * 2 + kh, kh, out[b], c.act_hi, c.act_lo, kh * KT, kh == 0, kh == 1)

            @block.scalar
            def _(act):
                act.sem_inc(half0, 2)
                act.wait_ge(fstep, 4)
                act.activation(e[:], e[:], ACT.Exp).then_inc(fact, 1)
                act.wait_ge(fact, 1)
                act.activation(lg[:], e[:], ACT.Ln, bias=1.0).then_inc(fact, 1)


                def evacuate(i, first):
                    for b in range(2):
                        m = i * 2 + b
                        act.wait_ge(ws.used, m * 2 + (2 + SPLIT))
                        if not first:
                            act.wait_ge(stored[b], i * 16)
                        act.activation(stage[:, b, 0:HALF], out[b][0], ACT.Copy).then_inc(half0, 1)
                        act.wait_ge(half0, m + 3)
                        act.wait_ge(half1, m + 3)
                        act.dma_start(proj[m], stage[:, b, :]).then_inc(stored[b], 16)

                first_then_loop(act, NM // 2, evacuate)
                for b in range(2):
                    act.wait_ge(stored[b], 16 * (NM // 2))

            @block.vector
            def _(dve):
                dve.wait_ge(small_in, 32)
                dve.tensor_copy(fw_hi[:], fw[:]).then_inc(fw_round, 1)
                dve.wait_ge(fw_round, 1)
                dve.tensor_tensor(fw_lo[:], fw[:], fw_hi[:].bitcast(F32), ALU.subtract).then_inc(fw_ready, 1)
                dve.sem_inc(half1, 2)
                dve.wait_ge(forget, 1)
                dve.tensor_tensor(z[:], c.bank[4][:, 0:TT * H].rearrange("p (t h) -> p t h", h=H),
                                  fb[:].unsqueeze(1).broadcast_to([P, TT, H]), ALU.add).then_inc(fstep, 1)
                dve.wait_ge(fstep, 1)
                dve.tensor_scalar(mn[:], z[:], 0.0, None, ALU.min).then_inc(fstep, 1)
                dve.tensor_scalar(e[:], z[:], 0.0, None, ALU.max).then_inc(fstep, 1)
                dve.wait_ge(fstep, 3)
                dve.tensor_tensor(e[:], mn[:], e[:], ALU.subtract).then_inc(fstep, 1)
                dve.wait_ge(fact, 2)
                dve.tensor_tensor(lg[:], mn[:], lg[:], ALU.subtract).then_inc(fstep, 1)

                def evacuate(i, first):
                    for b in range(2):
                        dve.wait_ge(ws.used, (i * 2 + b) * 2 + (2 + SPLIT))
                        if not first:
                            dve.wait_ge(stored[b], i * 16)
                        dve.tensor_copy(stage[:, b, HALF:T], out[b][1]).then_inc(half1, 1)

                first_then_loop(dve, NM // 2, evacuate)


def build_forget_sums(c, logf, cache_logf, negf_p, negf_s):
    nc = c.nc
    NK = PAST // P
    with ExitStack() as tmp:
        triangle = c.sb("triangle", [P, P + PAST], F32, tmp)
        lp = c.sb("logf_prompt", [P, TP // P, H], F32, tmp)
        ls = c.sb("logf_past", [P, NK, NB * H], F32, tmp)
        ln = c.sb("logf_new", [TS, NB, H], F32, tmp)
        out_p = c.sb("negf_p_sb", [H, TP], F32, tmp)
        out_s = c.sb("negf_s_sb", [NB * H, PAST + TS], F32, tmp)
        small_in, filled, made = c.sem("logf_in"), c.sem("triangle_filled"), c.sem("triangle_made")
        summed, copied, stored = c.sem("forget_summed"), c.sem("negf_copied"), c.sem("negf_stored")
        with nc.Block() as block:
            @block.gpsimd
            def _(pool):
                pool.memset(triangle[:], -1.0).then_inc(filled, 1)
                pool.wait_ge(filled, 1)
                pool.affine_select(out=triangle[:], in_=triangle[:], compare_op=ALU.is_ge, fill=0.0, base=0,
                                   pattern=[[1, P + PAST]], channel_multiplier=-1).then_inc(made, 1)

            @block.sync
            def _(sp):
                sp.dma_start(lp[:], logf[0:TP].rearrange("(t p) h -> p t h", p=P)).then_inc(small_in, 16)
                sp.dma_start(ls[:], cache_logf).then_inc(small_in, 16)
                sp.dma_start(ln[:], logf[TP:T].rearrange("(b i) h -> i b h", i=TS)).then_inc(small_in, 16)
                sp.wait_ge(copied, 2)
                sp.dma_start(negf_p, out_p[:]).then_inc(stored, 16)
                sp.dma_start(negf_s, out_s[:]).then_inc(stored, 16)
                sp.wait_ge(stored, 32)

            @block.tensor
            def _(pe):
                pe.wait_ge(small_in, 48)
                pe.wait_ge(made, 1)
                for k in reversed(range(TP // P)):
                    mm = pe.matmul(c.bank[3][0:H, k * P:TP], lp[:, k, :], triangle[:, 0:TP - k * P],
                                   start=(k == TP // P - 1), stop=(k == 0), skip_group_check=True)
                mm.then_inc(summed, 1)
                pe.matmul(c.bank[2][0:NB * H, 0:TS], ln[:].rearrange("i b h -> i (b h)"), triangle[0:TS, 0:TS],
                          start=True, stop=False, skip_group_check=True)
                for k in reversed(range(NK)):
                    for b, end in enumerate((512, 1024, PAST + TS)):
                        at = max(k * P, b * 512)
                        if at < end:
                            mm = pe.matmul(c.bank[b][0:NB * H, at - b * 512:end - b * 512], ls[:, k, :],
                                           triangle[:, at - k * P:end - k * P],
                                           start=(b < 2 and k == 4 * b + 3), stop=(k == 0), skip_group_check=True)
                mm.then_inc(summed, 1)

            @block.vector
            def _(dve):
                dve.wait_ge(summed, 1)
                dve.tensor_copy(out_p[:], c.bank[3][0:H, :]).then_inc(copied, 1)
                dve.wait_ge(summed, 2)
                for b in range(2):
                    dve.tensor_copy(out_s[:, b * 512:(b + 1) * 512], c.bank[b][0:NB * H, :])
                dve.tensor_copy(out_s[:, PAST:PAST + TS], c.bank[2][0:NB * H, 0:TS]).then_inc(copied, 1)


def build_prompt_attention(c, name, proj, base, yt, negf_p=None, rel=None):
    nc = c.nc
    NQ = TP // P
    with ExitStack() as tmp:
        qkv = c.sb(f"{name}_qkv", [P, 2, 3, TP], F32, tmp)
        q = c.sb(f"{name}_q", [P, 2, TP], F32, tmp)
        v = c.sb(f"{name}_v", [P, NQ, P], F32, tmp)
        prob = c.sb(f"{name}_prob", [P, NQ, TP], F32, tmp)
        prob_t = c.sb(f"{name}_prob_t", [P, NQ, TP], F32, tmp)
        stat = c.sb(f"{name}_stat", [P, 3, NQ], F32, tmp)
        y = c.sb(f"{name}_y", [P, 2, TP], F32, tmp)
        if rel is None:
            bias = c.sb(f"{name}_bias", [1, H * TP], F32, tmp)
        else:
            bias = c.sb(f"{name}_bias", [P, H, TP], F32, tmp)
        sem = {n: c.sem(f"{name}_{n}") for n in
               ("bias_in", "bias_ready", "q", "v_turned", "v", "scores", "maxed", "exped", "recip", "prob",
                "turned", "prob_t", "y_product", "y")}
        loaded = [c.sem(f"{name}_loaded{b}") for b in range(2)]
        stored = [c.sem(f"{name}_stored{b}") for b in range(2)]
        with nc.Block() as block:
            @block.sync
            def _(sp):
                if rel is None:
                    sp.dma_start(bias[:], negf_p.rearrange("h t -> (h t)").unsqueeze(0)).then_inc(sem["bias_in"], 16)
                else:
                    row = rel.shape[1]
                    sp.dma_start(bias[:], bass.AP(tensor=rel.tensor, offset=rel.offset + RPAD - (TP - P - REL) - (P - 1),
                                                  ap=[[1, P], [row, H], [1, TP]])).then_inc(sem["bias_in"], 16)

                def load(i, first):
                    for b in range(2):
                        if not first:
                            sp.wait_ge(sem["turned"], (i * 2 + (b - 2)) * NQ + NQ)
                        for j in range(3):
                            sp.dma_start(qkv[:, b, j], proj[i * 2 + (base + j * H + b), :, 0:TP]).then_inc(loaded[b], 16)

                first_then_loop(sp, H // 2, load)

            if rel is not None:
                @block.gpsimd
                def _(pool):
                    pool.wait_ge(sem["bias_in"], 16)
                    pool.memset(bias[P // 2:P, :, TP - P // 2:TP], NEG).then_inc(sem["bias_ready"], 1)

            @block.tensor
            def _(pe):
                if rel is None:
                    pe.wait_ge(sem["bias_in"], 16)
                else:
                    pe.wait_ge(sem["bias_ready"], 1)

                def head(i, first):
                    for b in range(2):
                        h = i * 2 + b
                        pe.wait_ge(loaded[b], i * 48 + 48)
                        pe.wait_ge(sem["q"], h + 1)
                        for t in range(NQ):
                            n = (t + 1) * P
                            if not (first and b == 0):
                                pe.wait_ge(sem["exped"], (h - 1) * NQ + (t + 1))
                            out = c.bank[t][:, 0:n]
                            if rel is None:
                                pe.matmul(c.bank[t][:, t * P:n], c.ident[:], c.causal[:], start=True, stop=False,
                                          skip_group_check=True)
                            pe.matmul(out, q[:, b, t * P:(t + 1) * P], qkv[:, b, 1, 0:n], start=(rel is not None), stop=False,
                                      skip_group_check=True)
                            if rel is None:
                                mm = pe.matmul(out, c.ones[0:1, :], bias[0:1, bass.ds(h * TP, n)], start=False, stop=True,
                                               skip_group_check=True)
                            else:
                                mm = pe.matmul(out, c.flip[:], bias[:, h, TP - n:TP], start=False, stop=True, skip_group_check=True)
                            mm.then_inc(sem["scores"], 1)
                        if not (first and b == 0):
                            values(h - 1, not (first and b == 1))
                        for k in range(NQ):
                            mm = pe.transpose(c.bank[4][:, k * P:(k + 1) * P], qkv[:, b, 2, k * P:(k + 1) * P], c.ident[:])
                        mm.then_inc(sem["v_turned"], 1)
                        for t in range(NQ):
                            r = h * NQ + t
                            pe.wait_ge(sem["prob"], r + 1)
                            if not (first and b == 0 and t < 2):
                                pe.wait_ge(sem["prob_t"], r - 1)
                            for k in range(t + 1):
                                mm = pe.transpose(c.bank[5 + t % 2][:, k * P:(k + 1) * P], prob[:, t, k * P:(k + 1) * P], c.ident[:])
                            mm.then_inc(sem["turned"], 1)

                def values(h, used):
                    pe.wait_ge(sem["prob_t"], h * NQ + NQ)
                    pe.wait_ge(sem["v"], h + 1)
                    if used:
                        pe.wait_ge(sem["y"], h)
                    for k in reversed(range(NQ)):
                        mm = pe.matmul(c.bank[7][:, k * P:TP], v[:, k, :], prob_t[:, k, k * P:TP],
                                       start=(k == NQ - 1), stop=(k == 0), skip_group_check=True)
                    mm.then_inc(sem["y_product"], 1)

                first_then_loop(pe, H // 2, head)
                values(H - 1, True)

            @block.scalar
            def _(act):
                def head(i, first):
                    for b in range(2):
                        h = i * 2 + b
                        for t in range(NQ):
                            r = h * NQ + t
                            act.wait_ge(sem["maxed"], r + 1)
                            if not (first and b == 0):
                                act.wait_ge(sem["turned"], r - (NQ - 1))
                            act.activation(prob[:, t, 0:(t + 1) * P], c.bank[t][:, 0:(t + 1) * P], ACT.Exp,
                                           bias=stat[:, 0, t:t + 1], accum_out=stat[:, 1, t:t + 1]).then_inc(sem["exped"], 1)
                        act.wait_ge(sem["v_turned"], h + 1)
                        act.activation(v[:], c.bank[4][:].rearrange("p (k d) -> p k d", d=P), ACT.Copy).then_inc(sem["v"], 1)
                        for t in range(NQ):
                            act.wait_ge(sem["turned"], h * NQ + (t + 1))
                            act.activation(prob_t[:, 0:t + 1, t * P:(t + 1) * P],
                                           c.bank[5 + t % 2][:, 0:(t + 1) * P].rearrange("p (k q) -> p k q", q=P),
                                           ACT.Copy).then_inc(sem["prob_t"], 1)

                first_then_loop(act, H // 2, head)

            @block.vector
            def _(dve):
                def head(i, first):
                    for b in range(2):
                        h = i * 2 + b
                        dve.wait_ge(loaded[b], i * 48 + 48)
                        dve.tensor_scalar(q[:, b], qkv[:, b, 0], QK_SCALE, None, ALU.mult).then_inc(sem["q"], 1)
                        for t in range(NQ):
                            dve.wait_ge(sem["scores"], h * NQ + (t + 1))
                            dve.tensor_reduce(stat[:, 0, t:t + 1], c.bank[t][:, 0:(t + 1) * P], AX.X, ALU.max,
                                              negate=True).then_inc(sem["maxed"], 1)
                        for t in range(NQ):
                            r = h * NQ + t
                            dve.wait_ge(sem["exped"], r + 1)
                            dve.reciprocal(stat[:, 2, t:t + 1], stat[:, 1, t:t + 1]).then_inc(sem["recip"], 1)
                            dve.wait_ge(sem["recip"], r + 1)
                            dve.tensor_scalar(prob[:, t, 0:(t + 1) * P], prob[:, t, 0:(t + 1) * P], stat[:, 2, t:t + 1],
                                              None, ALU.mult).then_inc(sem["prob"], 1)
                        if b == 1:
                            keep(h - 1, 0, i)
                        elif not first:
                            keep(h - 1, 1, i - 1)

                def keep(h, b, stores):
                    dve.wait_ge(sem["y_product"], h + 1)
                    if not (isinstance(stores, int) and stores == 0):
                        dve.wait_ge(stored[b], stores * 16)
                    dve.tensor_copy(y[:, b], c.bank[7][:]).then_inc(sem["y"], 1)

                head(0, True)
                head(1, False)
                with dve.Fori(2, H // 2) as i:
                    head(i, False)
                keep(H - 1, 1, H // 2 - 1)

            @block.gpsimd
            def _(pool):
                with pool.Fori(0, H // 2) as i:
                    for b in range(2):
                        pool.wait_ge(sem["y"], i * 2 + (b + 1))
                        pool.dma_start(yt[i * 2 + b, :, 0:TP], y[:, b]).then_inc(stored[b], 16)
                for b in range(2):
                    pool.wait_ge(stored[b], 16 * (H // 2))


def build_sample_attention(c, name, proj, base, yt, past, k_cache, v_cache, negf_s=None, rel=None):
    nc = c.nc
    L = past + TS
    NK = past // P
    NT = H * past // 2048
    PAIRS = H // 2
    PW = 2 * TS
    KV = NK // NT
    NBK = past // 512
    with ExitStack() as tmp:
        k_ring = c.sb(f"{name}_k_ring", [P, NT, PAIRS, 512], F32, tmp)
        v_ring = c.acc[:].rearrange("p k t -> p (k t)")[:, 0:NT * 2048].rearrange(
            "p (s b n) -> p s b n", s=NT, b=KV)
        new = c.sb(f"{name}_new", [P, 3, H, P], F32, tmp)
        q_pad = c.sb(f"{name}_q_pad", [P, H, P + TS], F32, tmp)
        k_new = c.sb(f"{name}_k_new", [P, H, TS], F32, tmp)
        v_new = c.sb(f"{name}_v_new", [P, H, TS], F32, tmp)
        v_rows = c.sb(f"{name}_v_rows", [TS, H * HD], F32, tmp)
        prob = c.sb(f"{name}_prob", [P, L], F32, tmp)
        prob_t = c.sb(f"{name}_prob_t", [P, NK + 1, P], F32, tmp)
        stat = c.sb(f"{name}_stat", [P, 3], F32, tmp)
        o_rows = c.sb(f"{name}_o_rows", [P, 2 * HD], F32, tmp)
        y = c.sb(f"{name}_y", [P, H, P], F32, tmp)
        if rel is None:
            bias = c.sb(f"{name}_bias", [H, L], F32, tmp)
        else:
            bias = c.sb(f"{name}_bias", [P, L], F32, tmp)
        sem = {n: c.sem(f"{name}_{n}") for n in
               ("new_in", "bias_in", "zeroed", "picked", "k_used", "v_used", "v_turned", "v_rows", "v_rows_used", "scores", "maxed",
                "exped", "recip", "prob", "turned", "prob_t", "o_rows", "o_turned", "y", "stored")}
        k_in = [c.sem(f"{name}_k_in{s}") for s in range(NT)]
        v_in = [c.sem(f"{name}_v_in{s}") for s in range(NT)]
        q_flat = q_pad[:].rearrange("p h n -> p (h n)")
        s_bank = lambda j: c.bank[j]
        with nc.Block() as block:
            @block.sync
            def _(sp):
                for j in range(3):
                    sp.dma_start(new[:, j], proj[base + j * H:base + (j + 1) * H, :, TP:T].rearrange(
                        "h p t -> p h t")).then_inc(sem["new_in"], 16)
                if rel is not None:
                    row = rel.shape[1]
                    for h in range(H):
                        sp.dma_start(bias[(H - 1 - h) * TS:(H - h) * TS, :],
                                     bass.AP(tensor=rel.tensor, offset=rel.offset + h * row + RPAD - (past - REL) - (TS - 1),
                                             ap=[[1, TS], [1, L]])).then_inc(sem["bias_in"], 16)

                def load_keys(b, first):
                    if rel is None:
                        if not first:
                            sp.wait_ge(sem["scores"], b)
                        sp.dma_start(bias[:], negf_s[b]).then_inc(sem["bias_in"], 16)
                    for s in range(NT):
                        if not first:
                            sp.wait_ge(sem["k_used"], b * NT + (s + 1 - NT))
                        sp.dma_start(k_ring[:, s].rearrange("p h n -> p (h n)"), k_cache[b * NT + s]).then_inc(k_in[s], 16)

                def load_values(b, first):
                    for s in range(NT):
                        if not first:
                            sp.wait_ge(sem["v_used"], b * NT + (s + 1 - NT))
                        sp.dma_start(v_ring[:, s].rearrange("p b n -> p (b n)"), v_cache[b * NT + s]).then_inc(v_in[s], 16)

                load_keys(0, True)
                load_keys(1, False)
                load_values(0, True)
                with sp.Fori(2, NB) as b:
                    load_keys(b, False)
                    load_values(b - 1, False)
                load_values(NB - 1, False)
                sp.wait_ge(sem["y"], NB)
                sp.dma_start(yt[:, :, TP:T].rearrange("h p t -> p h t"), y[:]).then_inc(sem["stored"], 16)
                sp.wait_ge(sem["stored"], 16)

            @block.gpsimd
            def _(pool):
                pool.memset(q_pad[:], 0.0).then_inc(sem["zeroed"], 1)

            @block.tensor
            def _(pe):
                if rel is not None:
                    pe.wait_ge(sem["bias_in"], 16 * H)

                def sequence(b, first):
                    pe.wait_ge(sem["picked"], b * 3 + 3)
                    def stationary(h):
                        return q_flat[:, h * P + h // 2 * PW:h * P + (h // 2 + 1) * PW]

                    for odd in range(2):
                        for g in range(PAIRS):
                            pe.matmul(s_bank(NBK)[g * PW:(g + 1) * PW, 0:TS], stationary(2 * g + odd), k_new[:, 2 * g + odd, :],
                                      start=(odd == 0), stop=False, skip_group_check=True)
                    for s in range(NT):
                        pe.wait_ge(k_in[s], b * 16 + 16)
                        for g in range(PAIRS):
                            mm = pe.matmul(s_bank(s // 2)[g * PW:(g + 1) * PW, :], stationary(2 * g + s % 2), k_ring[:, s, g, :],
                                           start=(s % 2 == 0), stop=False, skip_group_check=True)
                        mm.then_inc(sem["k_used"], 1)
                    if rel is None:
                        pe.wait_ge(sem["bias_in"], b * 16 + 16)
                    rows = c.head_rows[:].rearrange("k h i -> k (h i)") if rel is None else c.flip[:]
                    for j in range(NBK):
                        pe.matmul(s_bank(j)[:], rows, bias[:, j * 512:(j + 1) * 512], start=False, stop=True, skip_group_check=True)
                    mm = pe.matmul(s_bank(NBK)[:, 0:TS], rows, bias[:, past:L], start=False, stop=(rel is not None),
                                   skip_group_check=True)
                    if rel is None:
                        mm = pe.matmul(s_bank(NBK)[:, 0:TS], c.query_rows[:].rearrange("k h i -> k (h i)"),
                                       c.causal[0:TS, 0:TS], start=False, stop=True, skip_group_check=True)
                    mm.then_inc(sem["scores"], 1)
                    if not first:
                        pe.wait_ge(sem["prob_t"], b * (NBK + 1))
                    for h in range(H):
                        mm = pe.transpose(c.bank[3 + h // 4][0:TS, (h % 4) * HD:(h % 4 + 1) * HD], v_new[:, h, :], c.ident[:])
                    mm.then_inc(sem["v_turned"], 1)
                    if not first:
                        values(b - 1, b - 1)
                    pe.wait_ge(sem["prob"], b + 1)
                    pe.wait_ge(sem["v_rows"], b + 1)
                    for k in range(NK):
                        mm = pe.transpose(c.bank[3 + k // 4][:, (k % 4) * P:(k % 4 + 1) * P], prob[:, k * P:(k + 1) * P], c.ident[:])
                        if k % 4 == 3:
                            mm.then_inc(sem["turned"], 1)
                    pe.transpose(c.bank[5][0:TS, 0:P], prob[:, past:L], c.ident[:]).then_inc(sem["turned"], 1)
                    if not first:
                        turn_back(b - 1)

                def values(b, kept):
                    if not (isinstance(kept, int) and kept == 0):
                        pe.wait_ge(sem["y"], kept)
                        own_instruction(c, pe)
                    for n, k in enumerate([NK, *range(NK)]):
                        if k < NK and k % KV == 0:
                            pe.wait_ge(v_in[k // KV], b * 16 + 16)
                        for g in range(PAIRS):
                            pair, both = slice(g * PW, (g + 1) * PW), slice(2 * g * HD, 2 * (g + 1) * HD)
                            if k < NK:
                                lhs, rhs = prob_t[:, k, pair], v_ring[:, k // KV, k % KV, both]
                            else:
                                lhs, rhs = prob_t[0:TS, k, pair], v_rows[:, both]
                            mm = pe.matmul(c.bank[6][pair, 0:2 * HD], lhs, rhs, start=(n == 0), stop=(n == NK),
                                           skip_group_check=True)
                        if k == NK:
                            mm.then_inc(sem["v_rows_used"], 1)
                        elif k % KV == KV - 1:
                            mm.then_inc(sem["v_used"], 1)

                def turn_back(b):
                    pe.wait_ge(sem["o_rows"], b + 1)
                    for odd in range(2):
                        mm = pe.transpose(c.bank[7][:, odd * P:(odd + 1) * P], o_rows[:, odd * HD:(odd + 1) * HD], c.ident[:])
                    mm.then_inc(sem["o_turned"], 1)

                sequence(0, True)
                sequence(1, False)
                with pe.Fori(2, NB) as b:
                    sequence(b, False)
                pe.wait_ge(sem["prob_t"], NB * (NBK + 1))
                values(NB - 1, NB - 1)
                turn_back(NB - 1)

            @block.scalar
            def _(act):
                def sequence(b, first):
                    act.wait_ge(sem["maxed"], b + 1)
                    if not first:
                        act.wait_ge(sem["turned"], b * (NBK + 1))
                    act.activation(prob[:], c.scores[:, 0:L], ACT.Exp, bias=stat[:, 0:1],
                                   accum_out=stat[:, 1:2]).then_inc(sem["exped"], 1)
                    act.wait_ge(sem["v_turned"], b + 1)
                    if not first:
                        act.wait_ge(sem["v_rows_used"], b)
                    act.activation(v_rows[:, 0:512], c.bank[3][0:TS, :], ACT.Copy)
                    act.activation(v_rows[:, 512:1024], c.bank[4][0:TS, :], ACT.Copy).then_inc(sem["v_rows"], 1)
                    for j in range(NBK):
                        act.wait_ge(sem["turned"], b * (NBK + 1) + (j + 1))
                        act.activation(prob_t[:, 4 * j:4 * j + 4, :].rearrange("p k q -> p (k q)"), c.bank[3 + j][:],
                                       ACT.Copy).then_inc(sem["prob_t"], 1)
                    act.wait_ge(sem["turned"], b * (NBK + 1) + (NBK + 1))
                    act.activation(prob_t[0:TS, NK, :], c.bank[5][0:TS, 0:P], ACT.Copy).then_inc(sem["prob_t"], 1)

                first_then_loop(act, NB, sequence)

            @block.vector
            def _(dve):
                dve.wait_ge(sem["new_in"], 48)
                dve.wait_ge(sem["zeroed"], 1)

                def pick(b, first):
                    if not first:
                        dve.wait_ge(sem["v_turned"], b)
                    at = bass.ds(b * TS, TS)
                    dve.tensor_scalar(q_pad[:, :, 0:TS], new[:, 0, :, at], QK_SCALE, None, ALU.mult).then_inc(sem["picked"], 1)
                    dve.tensor_copy(k_new[:], new[:, 1, :, at]).then_inc(sem["picked"], 1)
                    dve.tensor_copy(v_new[:], new[:, 2, :, at]).then_inc(sem["picked"], 1)

                def softmax(b):
                    dve.wait_ge(sem["scores"], b + 1)
                    dve.tensor_reduce(stat[:, 0:1], c.scores[:, 0:L], AX.X, ALU.max, negate=True).then_inc(sem["maxed"], 1)
                    dve.wait_ge(sem["exped"], b + 1)
                    dve.reciprocal(stat[:, 2:3], stat[:, 1:2]).then_inc(sem["recip"], 1)
                    dve.wait_ge(sem["recip"], b + 1)
                    dve.tensor_scalar(prob[:], prob[:], stat[:, 2:3], None, ALU.mult).then_inc(sem["prob"], 1)

                def rows_of(b):
                    dve.wait_ge(sem["v_used"], b * NT + NT)
                    dve.tensor_copy(o_rows[:], c.bank[6][:, 0:2 * HD]).then_inc(sem["o_rows"], 1)

                def keep(b):
                    dve.wait_ge(sem["o_turned"], b + 1)
                    pairs_of = y[:, :, bass.ds(b * TS, TS)].rearrange("p (g r) i -> p g r i", r=2)
                    for odd in range(2):
                        turned = c.bank[7][:, odd * P:(odd + 1) * P].rearrange("p (g r i) -> p g r i", r=2, i=TS)
                        op = dve.tensor_copy(pairs_of[:, :, odd], turned[:, :, odd])
                    op.then_inc(sem["y"], 1)

                pick(0, True)
                softmax(0)
                pick(1, False)
                softmax(1)
                rows_of(0)
                with dve.Fori(2, NB) as b:
                    pick(b, False)
                    keep(b - 2)
                    softmax(b)
                    rows_of(b - 1)
                keep(NB - 2)
                rows_of(NB - 1)
                keep(NB - 1)


class Residual:

    def __init__(self, c, tmp, name, row):
        self.c, self.row = c, row
        self.sample = c.sb(f"{name}_sample", [P, NB, TS], F32, tmp)
        self.scaled, self.added = c.sem(f"{name}_scaled"), c.sem(f"{name}_added")

    def add(self, dve, n, m, out):
        c, gate = self.c, lambda lo, hi: self.c.ada[:, m + self.row * DC, lo:hi]
        tail = out[1][:, TP - HALF:HALF].rearrange("p (b i) -> p b i", i=TS)
        acc_tail = c.acc[:, m, TP:T].rearrange("p (b i) -> p b i", i=TS)
        dve.wait_ge(self.added, n + 2)
        dve.tensor_tensor(self.sample[:], tail, gate(1, NC9).unsqueeze(2).broadcast_to([P, NB, TS]),
                          ALU.mult).then_inc(self.scaled, 1)
        dve.scalar_tensor_tensor(out=c.acc[:, m, 0:HALF], in0=out[0], scalar=gate(0, 1),
                                 in1=c.acc[:, m, 0:HALF], op0=ALU.mult, op1=ALU.add)
        dve.scalar_tensor_tensor(out=c.acc[:, m, HALF:TP], in0=out[1][:, 0:TP - HALF], scalar=gate(0, 1),
                                 in1=c.acc[:, m, HALF:TP], op0=ALU.mult, op1=ALU.add)
        dve.wait_ge(self.scaled, n + 1)
        dve.tensor_tensor(acc_tail, acc_tail, self.sample[:], ALU.add).then_inc(self.added, 1)


def build_merge(c, name, tiles, yt, first_branch):
    nc = c.nc
    with ExitStack() as tmp:
        ws = WeightStream(c, tmp, name)
        y_hi = c.sb(f"{name}_y_hi", [P, H, T], F32R, tmp)
        y_lo = c.sb(f"{name}_y_lo", [P, H, T], F32R, tmp)
        work = c.sb(f"{name}_work", [P, 2, T], F32, tmp)
        y_in = [c.sem(f"{name}_y_in{b}") for b in range(2)]
        hi, lo, gate, scaled, merged = (c.sem(f"{name}_{n}") for n in ("hi", "lo", "gate", "scaled", "merged"))
        with nc.Block() as block:
            @block.sync
            def _(sp):
                ws.load(sp, tiles, 3 * DC)

            @block.gpsimd
            def _(pool):
                ws.divide(pool, 3 * DC)

            @block.scalar
            def _(act):
                def split(h):
                    act.wait_ge(y_in[h % 2], 16 * (h // 2 + 1))
                    act.activation(y_hi[:, h], work[:, h % 2], ACT.Copy).then_inc(hi, 1)

                for h in range(H):
                    if h >= 2:
                        act.wait_ge(lo, h - 1)
                    act.dma_start(work[:, h % 2], yt[h]).then_inc(y_in[h % 2], 16)
                    if h >= 1:
                        split(h - 1)
                split(H - 1)
                act.wait_ge(lo, H)
                with act.Fori(0, DC // 2) as i:
                    for b in range(2):
                        m = i * 2 + b
                        act.wait_ge(ws.used, m * 3 + (3 + SPLIT))
                        act.wait_ge(merged, m + 1)
                        for j in range(2):
                            act.activation(work[:, b, j * HALF:(j + 1) * HALF], c.halves(4 * b + 2)[j],
                                           ACT.Sigmoid).then_inc(gate, 1)

            @block.tensor
            def _(pe):
                def columns(i, first):
                    for b in range(2):
                        m = i * 2 + b
                        pe.wait_ge(merged, m + 1)
                        for j in range(3):
                            n = m * 3 + j
                            if j == 2:
                                ws.multiply(pe, n, (3 * b + j) % 2, c.halves(4 * b), y_hi, y_lo, 0, True, True,
                                            chunk_ready=lo if first and b == 0 else None)
                            else:
                                ws.multiply(pe, n, (3 * b + j) % 2, c.halves(4 * b + 2), c.act_hi, c.act_lo,
                                            j * KT, j == 0, j == 1)

                first_then_loop(pe, DC // 2, columns)

            @block.vector
            def _(dve):
                dve.sem_inc(merged, 2)
                for h in range(H):
                    dve.wait_ge(hi, h + 1)
                    dve.tensor_tensor(y_lo[:, h], work[:, h % 2], y_hi[:, h].bitcast(F32), ALU.subtract).then_inc(lo, 1)
                with dve.Fori(0, DC // 2) as i:
                    for b in range(2):
                        m = i * 2 + b
                        dve.wait_ge(gate, m * 2 + 2)
                        out = c.halves(4 * b)
                        for j in range(2):
                            at = slice(j * HALF, (j + 1) * HALF)
                            dst = c.acc[:, m, at] if first_branch else work[:, b, at]
                            op = dve.tensor_tensor(dst, out[j], work[:, b, at], ALU.mult)
                        if first_branch:
                            op.then_inc(merged, 1)
                        else:
                            op.then_inc(scaled, 1)
                            dve.wait_ge(scaled, m + 1)
                            dve.tensor_tensor(c.acc[:, m], c.acc[:, m], work[:, b], ALU.add).then_inc(merged, 1)


def build_output(c, tiles, x_dram):
    nc = c.nc
    with ExitStack() as tmp:
        ws = WeightStream(c, tmp, "out")
        res = Residual(c, tmp, "out_res", 2)
        hi, lo = c.sem("merged_hi"), c.sem("merged_lo")
        x_in = c.sem("out_x_in")
        with nc.Block() as block:
            @block.sync
            def _(sp):
                ws.load(sp, tiles, 2 * DC)

            @block.gpsimd
            def _(pool):
                ws.divide(pool, 2 * DC)

            @block.scalar
            def _(act):
                for k in range(DC):
                    act.activation(c.act_hi[:, k], c.acc[:, k], ACT.Copy).then_inc(hi, 1)
                act.wait_ge(lo, DC)
                act.dma_start(c.acc[:], x_dram.rearrange("k p t -> p k t")).then_inc(x_in, 16)

            @block.tensor
            def _(pe):
                def columns(i, first):
                    for b in range(2):
                        m = i * 2 + b
                        pe.wait_ge(res.added, m + 1)
                        for kh in range(2):
                            ws.multiply(pe, m * 2 + kh, kh, c.halves(2 * b), c.act_hi, c.act_lo, kh * KT, kh == 0,
                                        kh == 1, chunk_ready=lo if first and b == 0 else None)

                first_then_loop(pe, DC // 2, columns)

            @block.vector
            def _(dve):
                dve.sem_inc(res.added, 2)
                for k in range(DC):
                    dve.wait_ge(hi, k + 1)
                    dve.tensor_tensor(c.act_lo[:, k], c.acc[:, k], c.act_hi[:, k].bitcast(F32),
                                      ALU.subtract).then_inc(lo, 1)
                dve.wait_ge(x_in, 16)
                with dve.Fori(0, DC // 2) as i:
                    for b in range(2):
                        m = i * 2 + b
                        dve.wait_ge(ws.used, m * 2 + (2 + SPLIT))
                        res.add(dve, m, m, c.halves(2 * b))


def build_retrieval(c, tiles, sub_keys, key1_t, key2_t, gate_t):
    nc = c.nc
    NHD = H // 2
    with ExitStack() as tmp:
        ws = WeightStream(c, tmp, "query")
        keys = c.sb("sub_keys_sb", [P, 2 * H, NKEY], F32, tmp)
        query = c.sb("query_sb", [P, 2, T], F32, tmp)
        score = c.sb("key_scores", [P, 2, TT, 2, NKEY], F32, tmp)
        rest = c.sb("scores_rest", [P, TT, 2, NKEY], F32, tmp)
        top = c.sb("top_keys", [P, TT, 2, TOPK], F32, tmp)
        top_at = c.sb("top_keys_at", [P, TT, 2, TOPK], U32, tmp)
        top_atf = c.sb("top_keys_atf", [P, TT, 2, TOPK], F32, tmp)
        cand = c.sb("candidates", [P, TT, TOPK, TOPK], F32, tmp)
        crest = rest[:].rearrange("p t c n -> p t (c n)")
        best = c.sb("best", [P, TT, TOPK], F32, tmp)
        best_at = c.sb("best_at", [P, TT, TOPK], U32, tmp)
        rank_at = cand[:].rearrange("p t a b -> p (t a b)")[:, 0:2 * TT * TOPK].bitcast(U32).rearrange(
            "p (s t k) -> p s t k", s=2, t=TT)
        rank = c.sb("rank", [P, 2, TT, TOPK], F32, tmp)
        shifted = c.sb("best_shifted", [P, TT, TOPK], F32, tmp)
        total = c.sb("gate_total", [P, 2, TT], F32, tmp)
        found = [out[:].rearrange("p (t k) -> p t k", k=H * TOPK) for out in (key1_t, key2_t, gate_t)]
        keys_in, query_ready = c.sem("sub_keys_in"), c.sem("query_ready")
        scored, score_ready, score_free = c.sem("scored"), c.sem("score_ready"), c.sem("score_free")
        step, expd, turned = c.sem("topk_step"), c.sem("gate_exp"), c.sem("found_turned")
        gate_ready = c.sem("gate_t_ready")
        STEPS = 21
        with nc.Block() as block:
            @block.sync
            def _(sp):
                sp.dma_start(keys[:], sub_keys).then_inc(keys_in, 16)
                ws.load(sp, tiles, 2 * DC)

            @block.gpsimd
            def _(pool):
                ws.divide(pool, 2 * DC)

            @block.tensor
            def _(pe):
                def score_of(m, b):
                    pe.wait_ge(query_ready, m * 2 + 2)
                    pe.wait_ge(score_ready, m + 1)
                    for t in range(TT):
                        mm = pe.matmul(c.bank[4 + t // 4][:, (t % 4) * P:(t % 4 + 1) * P],
                                       query[:, b, t * P:(t + 1) * P], keys[:, m, :], start=True, stop=True)
                    mm.then_inc(scored, 1)

                def columns(i, first):
                    for b in range(2):
                        m = i * 2 + b
                        if not first:
                            pe.wait_ge(query_ready, m * 2 - 2)
                        for kh in range(2):
                            ws.multiply(pe, m * 2 + kh, kh, c.halves(2 * b), c.act_hi, c.act_lo, kh * KT, kh == 0, kh == 1)
                        if not (first and b == 0):
                            score_of(m - 1, 1 - b)

                pe.wait_ge(keys_in, 16)
                first_then_loop(pe, DC // 2, columns)
                score_of(DC - 1, 1)
                pe.wait_ge(step, H * STEPS)
                for j in range(3):
                    for t in range(TT):
                        mm = pe.transpose(c.bank[2 * j + t // 4][:, (t % 4) * P:(t % 4 + 1) * P], found[j][:, t, :], c.ident[:])
                    mm.then_inc(turned, 1)

            @block.scalar
            def _(act):
                def evacuate(m, b, first):
                    act.wait_ge(ws.used, m * 2 + (2 + SPLIT))
                    if not first:
                        act.wait_ge(scored, m - 1)
                    for j in range(2):
                        act.activation(query[:, b, j * HALF:(j + 1) * HALF], c.halves(2 * b)[j],
                                       ACT.Copy).then_inc(query_ready, 1)

                def keep(m, hb, side):
                    act.wait_ge(scored, m + 1)
                    act.activation(score[:, hb, 0:4, side, :], c.bank[4][:].rearrange("p (t n) -> p t n", n=NKEY), ACT.Copy)
                    act.activation(score[:, hb, 4, side, :], c.bank[5][:, 0:NKEY], ACT.Copy).then_inc(score_ready, 1)

                def head_exp(h):
                    act.wait_ge(step, h * STEPS + 10)
                    act.activation(shifted[:], shifted[:], ACT.Exp).then_inc(expd, 1)

                def two_heads(i, first):
                    for hb in range(2):
                        h = i * 2 + hb
                        for side in range(2):
                            m = h * 2 + side
                            evacuate(m, side, first and hb == 0)
                            if side == 1:
                                act.wait_ge(score_free, h + 1)
                                keep(m - 1, hb, 0)
                            elif not (first and hb == 0):
                                keep(m - 1, 1 - hb, 1)
                                if not (first and hb == 1):
                                    head_exp(h - 2)

                act.sem_inc(score_ready, 1)
                first_then_loop(act, NHD, two_heads)
                keep(DC - 1, 1, 1)
                head_exp(H - 2)
                head_exp(H - 1)

            @block.vector
            def _(dve):
                dve.sem_inc(score_free, 2)

                def retrieve(i, first):
                    for hb in range(2):
                        head(i * 2 + hb, hb)

                def head(h, hb):
                    def done(k, searches=False):
                        dve.wait_ge(step, h * STEPS + k)
                        if searches:
                            own_instruction(c, dve)

                    pairs = [(t, s) for t in range(TT) for s in range(2)]
                    dve.wait_ge(score_ready, h * 2 + 3)
                    own_instruction(c, dve)
                    for t, s in pairs:
                        op = dve.max(top[:, t, s, 0:8], score[:, hb, t, s, :])
                    op.then_inc(step, 1)
                    done(1, searches=True)
                    for t, s in pairs:
                        dve.max_index(top_at[:, t, s, 0:8], top[:, t, s, 0:8], score[:, hb, t, s, :])
                        op = dve.match_replace(rest[:, t, s, :], top[:, t, s, 0:8], score[:, hb, t, s, :], LOWEST)
                    op.then_inc(step, 1)
                    done(2, searches=True)
                    for t, s in pairs:
                        op = dve.max(top[:, t, s, 8:16], rest[:, t, s, :])
                    op.then_inc(step, 1)
                    done(3, searches=True)
                    dve.sem_inc(score_free, 1)
                    for t, s in pairs:
                        op = dve.max_index(top_at[:, t, s, 8:16], top[:, t, s, 8:16], rest[:, t, s, :])
                    op.then_inc(step, 1)
                    done(4)
                    dve.tensor_copy(top_atf[:], top_at[:])
                    dve.tensor_tensor(cand[:], top[:, :, 0, :].unsqueeze(3).broadcast_to([P, TT, TOPK, TOPK]),
                                      top[:, :, 1, :].unsqueeze(2).broadcast_to([P, TT, TOPK, TOPK]),
                                      ALU.add).then_inc(step, 1)
                    done(5, searches=True)
                    flat = cand[:].rearrange("p t a b -> p t (a b)")
                    for t in range(TT):
                        op = dve.max(best[:, t, 0:8], flat[:, t, :])
                    op.then_inc(step, 1)
                    done(6, searches=True)
                    for t in range(TT):
                        dve.max_index(best_at[:, t, 0:8], best[:, t, 0:8], flat[:, t, :])
                        op = dve.match_replace(crest[:, t, :], best[:, t, 0:8], flat[:, t, :], LOWEST)
                    op.then_inc(step, 1)
                    done(7, searches=True)
                    for t in range(TT):
                        op = dve.max(best[:, t, 8:16], crest[:, t, :])
                    op.then_inc(step, 1)
                    done(8, searches=True)
                    for t in range(TT):
                        op = dve.max_index(best_at[:, t, 8:16], best[:, t, 8:16], crest[:, t, :])
                    op.then_inc(step, 1)
                    done(9)
                    dve.tensor_tensor(shifted[:], best[:], best[:, :, 0:1].broadcast_to([P, TT, TOPK]),
                                      ALU.subtract).then_inc(step, 1)
                    dve.tensor_scalar(rank_at[:, 0], best_at[:], 4, None, ALU.logical_shift_right)
                    dve.tensor_scalar(rank_at[:, 1], best_at[:], TOPK - 1, None, ALU.bitwise_and).then_inc(step, 1)
                    done(11)
                    dve.tensor_copy(rank[:], rank_at).then_inc(step, 1)
                    done(12)
                    for s in range(2):
                        dve.tensor_tensor(cand[:], c.iota[:, 0:TOPK].unsqueeze(1).unsqueeze(1).broadcast_to([P, TT, TOPK, TOPK]),
                                          rank[:, s].unsqueeze(3).broadcast_to([P, TT, TOPK, TOPK]),
                                          ALU.is_equal).then_inc(step, 1)
                        done(13 + 3 * s)
                        dve.tensor_tensor(cand[:], cand[:], top_atf[:, :, s, :].unsqueeze(2).broadcast_to([P, TT, TOPK, TOPK]),
                                          ALU.mult).then_inc(step, 1)
                        done(14 + 3 * s)
                        dve.tensor_reduce(found[s][:, :, bass.ds(h * TOPK, TOPK)], cand[:], AX.X, ALU.add).then_inc(step, 1)
                        done(15 + 3 * s)
                    dve.wait_ge(expd, h + 1)
                    dve.tensor_reduce(total[:, 0], shifted[:], AX.X, ALU.add).then_inc(step, 1)
                    done(19)
                    dve.reciprocal(total[:, 1], total[:, 0]).then_inc(step, 1)
                    done(20)
                    dve.tensor_tensor(found[2][:, :, bass.ds(h * TOPK, TOPK)], shifted[:],
                                      total[:, 1].unsqueeze(2).broadcast_to([P, TT, TOPK]), ALU.mult).then_inc(step, 1)
                    done(21)

                first_then_loop(dve, NHD, retrieve)
                for j, out in enumerate((key1_t, key2_t, gate_t)):
                    dve.wait_ge(turned, j + 1)
                    dve.tensor_copy(out[:, 0:512], c.bank[2 * j][:])
                    op = dve.tensor_copy(out[:, 512:T], c.bank[2 * j + 1][:, 0:T - 512])
                op.then_inc(gate_ready, 1)
                dve.wait_ge(gate_ready, 1)


def build_gates(c, key1_t, key2_t, gate_t, gates):
    nc = c.nc
    Q = 4
    NQ = GB // Q
    SLOTS = 4
    AHEAD = 2
    with ExitStack() as tmp:
        gate_hi, gate_lo = (c.sb(f"gate_{n}", [P, T], F32R, tmp) for n in ("hi", "lo"))
        rounded = c.sem("gates_rounded")
        gbuf = c.sb("gate_batch", [P, 2, NKEY, GB], F32, tmp)
        second = [c.sb(f"onehot_second{s}", [P, Q, NKEY], F32, tmp) for s in range(SLOTS)]
        onehot = [c.sb(f"onehot{s}", [P, Q, NKEY], F32R, tmp) for s in range(SLOTS)]
        wide_hi = [c.sb(f"gated_hi{s}", [P, Q, NKEY], F32R, tmp) for s in range(SLOTS)]
        wide_lo = [c.sb(f"gated_lo{s}", [P, Q, NKEY], F32R, tmp) for s in range(SLOTS)]
        sel, gated, low, both, product, kept = (
            c.sem(f"gates_{n}") for n in ("sel", "gated", "low", "both", "product", "kept"))
        stored = [c.sem(f"gates_stored{b}") for b in range(2)]

        def act_share(s):
            return Q if s % 2 == 0 else Q // 2

        def of(v, n, lo=0, hi=Q):
            return v[:, bass.ds(n * Q + lo, hi - lo)].unsqueeze(2).broadcast_to([P, hi - lo, NKEY])

        with nc.Block() as block:
            @block.gpsimd
            def _(pool):
                with pool.Fori(0, T // Q // SLOTS) as i:
                    for s in range(SLOTS):
                        n = i * SLOTS + s
                        pool.wait_ge(sel, n + 1)
                        pool.tensor_tensor(wide_hi[s][:], second[s][:], of(gate_hi[:].bitcast(F32), n),
                                           ALU.mult).then_inc(gated, 1)

            @block.vector
            def _(dve):
                dve.tensor_copy(gate_hi[:], gate_t[:]).then_inc(rounded, 1)
                dve.wait_ge(rounded, 1)
                dve.tensor_tensor(gate_lo[:], gate_t[:], gate_hi[:].bitcast(F32), ALU.subtract).then_inc(rounded, 1)
                dve.wait_ge(rounded, 2)
                dve.sem_inc(product, SLOTS)
                every = c.iota[:].unsqueeze(1).broadcast_to([P, Q, NKEY])
                with dve.Fori(0, T // Q // SLOTS) as i:
                    for s in range(SLOTS):
                        n = i * SLOTS + s
                        dve.wait_ge(product, n + 1)
                        dve.tensor_tensor(second[s][:], every, of(key2_t, n), ALU.is_equal).then_inc(sel, 1)
                        op = dve.tensor_tensor(onehot[s][:], every, of(key1_t, n), ALU.is_equal)
                        mine = act_share(s)
                        if mine < Q:
                            dve.wait_ge(sel, n + 1)
                            op = dve.tensor_tensor(wide_lo[s][:, mine:Q], second[s][:, mine:Q],
                                                   of(gate_lo[:].bitcast(F32), n, mine), ALU.mult)
                        op.then_inc(both, 1)

            @block.tensor
            def _(pe):
                with pe.Fori(0, T // Q // SLOTS) as i:
                    for s in range(SLOTS):
                        n = i * SLOTS + s
                        pe.wait_ge(both, n + 1)
                        pe.wait_ge(gated, n + 1)
                        pe.wait_ge(low, n + 1)
                        pe.wait_ge(kept, n + 1)
                        for j in range(Q):
                            out = c.bank[s][:, j * NKEY:(j + 1) * NKEY]
                            pe.matmul(out, onehot[s][:, j, :], wide_hi[s][:, j, :], start=True, stop=False)
                            mm = pe.matmul(out, onehot[s][:, j, :], wide_lo[s][:, j, :], start=False, stop=True)
                        mm.then_inc(product, 1)

            @block.scalar
            def _(act):
                def make_low(n, s):
                    act.wait_ge(sel, n + 1)
                    for j in range(act_share(s)):
                        op = act.activation(wide_lo[s][:, j, :], second[s][:, j, :], ACT.Copy,
                                            scale=gate_lo[:, bass.ds(n * Q + j, 1)].bitcast(F32))
                    op.then_inc(low, 1)

                def keep(b, q, n, s):
                    act.wait_ge(product, n + (1 + SLOTS))
                    act.activation(gbuf[:, b, :, bass.ds(q * Q, Q)].rearrange("p c t -> p t c"),
                                   c.bank[s][:].rearrange("p (t c) -> p t c", c=NKEY), ACT.Copy).then_inc(kept, 1)

                def batch(i, b, last):
                    whole = NQ // SLOTS - (1 if last else 0)
                    with act.Fori(0, whole) as r:
                        for s in range(SLOTS):
                            n = (i * 2 + b) * NQ + (r * SLOTS + s)
                            make_low(n + AHEAD, (s + AHEAD) % SLOTS)
                            keep(b, r * SLOTS + s, n, s)
                    if last:
                        for q in range(whole * SLOTS, NQ):
                            n = (i * 2 + b) * NQ + q
                            if q < NQ - AHEAD:
                                make_low(n + AHEAD, (q + AHEAD) % SLOTS)
                            keep(b, q, n, q % SLOTS)

                def batches(i, first, last=False):
                    for b in range(2):
                        if not first:
                            act.wait_ge(stored[b], i * 16)
                        batch(i, b, last and b == 1)

                act.sem_inc(kept, SLOTS)
                for n in range(AHEAD):
                    make_low(n, n)
                batches(0, True)
                with act.Fori(1, NGB // 2 - 1) as i:
                    batches(i, False)
                batches(NGB // 2 - 1, False, last=True)

            @block.sync
            def _(sp):
                with sp.Fori(0, NGB // 2) as i:
                    for b in range(2):
                        sp.wait_ge(kept, (i * 2 + b) * NQ + (NQ + SLOTS))
                        sp.dma_start(gates[i * 2 + b], gbuf[:, b]).then_inc(stored[b], 16)
                for b in range(2):
                    sp.wait_ge(stored[b], 16 * (NGB // 2))


def build_experts(c, tiles, gates):
    nc = c.nc
    NU = 2 * GROUP
    NV = DC
    with ExitStack() as tmp:
        ws = WeightStream(c, tmp, "expert")
        res = Residual(c, tmp, "expert_res", 5)
        w_hi = c.sb("gated_act_hi", [P, GROUP, T], F32R, tmp)
        w_lo = c.sb("gated_act_lo", [P, GROUP, T], F32R, tmp)
        gate = c.sb("gate_chunk", [P, 2, T], F32, tmp)
        hidden = c.sb("hidden", [P, T], F32, tmp)
        gate_in = [c.sem(f"expert_gate_in{b}") for b in range(2)]
        gelu, gated, hi, lo = (c.sem(f"expert_{n}") for n in ("gelu", "gated", "hi", "lo"))
        with nc.Block() as block:
            @block.sync
            def _(sp):
                with sp.Fori(0, NGROUP) as g:
                    with sp.Fori(0, NU // RAW) as i:
                        ws.load_four(sp, tiles, g * (NU + NV) + i * RAW)
                    with sp.Fori(0, NV // RAW) as i:
                        ws.load_four(sp, tiles, g * (NU + NV) + (i * RAW + NU))

            @block.gpsimd
            def _(pool):
                ws.divide(pool, NGROUP * (NU + NV))

            @block.tensor
            def _(pe):
                with pe.Fori(0, NGROUP) as g:
                    with pe.Fori(0, GROUP // 2) as i:
                        for b in range(2):
                            j = i * 2 + b
                            pe.wait_ge(gelu, (g * GROUP + j) * 2 + 2)
                            for kh in range(2):
                                ws.multiply(pe, g * (NU + NV) + j * 2 + kh, kh, c.halves(2 * b), c.act_hi, c.act_lo,
                                            kh * KT, kh == 0, kh == 1)

                    def sums(i, first):
                        for b in range(2):
                            m = i * 2 + b
                            pe.wait_ge(res.added, g * NV + m + 1)
                            ws.multiply(pe, g * (NU + NV) + (m + NU), b, c.halves(4 + 2 * b), w_hi, w_lo, 0, True, True,
                                        chunk_ready=lo if first and b == 0 else None,
                                        ready_from=g * GROUP + 1)

                    first_then_loop(pe, NV // 2, sums)

            @block.scalar
            def _(act):
                act.sem_inc(gelu, 4)
                with act.Fori(0, NGROUP) as g:
                    with act.Fori(0, GROUP // 2) as i:
                        for b in range(2):
                            j = i * 2 + b
                            n = g * GROUP + j
                            act.wait_ge(gated, n + 1)
                            act.dma_start(gate[:, b].rearrange("p (q t) -> p q t", t=GB),
                                          gates[:, :, n, :].rearrange("q p t -> p q t")).then_inc(gate_in[b], 16)
                            act.wait_ge(ws.used, g * (NU + NV) + j * 2 + (2 + SPLIT))
                            act.wait_ge(lo, n + 1)
                            for h in range(2):
                                act.activation(hidden[:, h * HALF:(h + 1) * HALF], c.halves(2 * b)[h],
                                               ACT.Gelu).then_inc(gelu, 1)
                            act.wait_ge(gated, n + 3)
                            act.activation(w_hi[:, j], hidden[:], ACT.Copy).then_inc(hi, 1)

            @block.vector
            def _(dve):
                dve.sem_inc(gated, 2)
                dve.sem_inc(lo, 1)
                dve.sem_inc(res.added, 2)
                with dve.Fori(0, NGROUP) as g:
                    with dve.Fori(0, GROUP // 2) as i:
                        for b in range(2):
                            j = i * 2 + b
                            n = g * GROUP + j
                            dve.wait_ge(gelu, n * 2 + (2 + 4))
                            dve.wait_ge(gate_in[b], (g * (GROUP // 2) + i) * 16 + 16)
                            dve.tensor_tensor(hidden[:], hidden[:], gate[:, b], ALU.mult).then_inc(gated, 1)
                            dve.wait_ge(hi, n + 1)
                            dve.tensor_tensor(w_lo[:, j], hidden[:], w_hi[:, j].bitcast(F32), ALU.subtract).then_inc(lo, 1)
                    with dve.Fori(0, NV // 2) as i:
                        for b in range(2):
                            m = i * 2 + b
                            dve.wait_ge(ws.used, g * (NU + NV) + m + (NU + 1 + SPLIT))
                            res.add(dve, g * NV + m, m, c.halves(4 + 2 * b))


def tiles_of(w):
    d, m = w.shape
    kh = d // (KT * P)
    return np.ascontiguousarray(w.reshape(kh, KT, P, m // P, P).transpose(3, 0, 2, 1, 4)).reshape(
        m // P * kh, P, KT * P)


def lay_out(a):
    feature_major = lambda v: np.ascontiguousarray(v.reshape(-1, P).T)
    chunked = lambda v: np.ascontiguousarray(v.T.reshape(DC, P, -1))
    x = np.concatenate([a["x_prompt"][0], a["x_sample"].reshape(NB * TS, D)])
    cond = np.concatenate([a["c_prompt"], a["c_sample"]])
    w_in = a["w_in"][0]
    f0, f1 = 3 * H * HD, 3 * H * HD + H
    g0 = f1 + 3 * H * HD
    gates = [tiles_of(w_in[:, g0 + r * D:g0 + (r + 1) * D]).reshape(DC, 2, P, KT * P) for r in range(2)]
    branches = [tiles_of(a[n][0]).reshape(DC, 1, P, KT * P) for n in ("w_branch_fox", "w_branch_band")]
    return {
        "x": chunked(x),
        "cond": np.pad(cond.T.reshape(DC, P, NC9).transpose(1, 0, 2), ((0, 0), (0, 0), (0, QUAD - NC9))),
        "w_ada": np.ascontiguousarray(a["w_ada"][0].reshape(RAW, DC // RAW, P, 6 * D // 512, 512).transpose(
            3, 0, 2, 1, 4)).reshape(6 * D // 512 * RAW, P, DC // RAW, 512),
        "b_ada": feature_major(a["b_ada"][0]),
        "norm_mix": feature_major(a["norm_mix"][0]),
        "norm_ffn": feature_major(a["norm_ffn"][0]),
        "norm_final": feature_major(a["norm_final"]),
        "w_heads": tiles_of(np.concatenate([w_in[:, :f0], w_in[:, f1:g0]], axis=1)),
        "cache_logf": np.ascontiguousarray(a["cache_fox_logf"][0].reshape(NB, PAST // P, P, H).transpose(
            2, 1, 0, 3)).reshape(P, PAST // P, NB * H),
        "fox_k": np.ascontiguousarray(a["cache_fox_k"][0].reshape(NB, 2, 512, 4, 2, HD).transpose(
            0, 1, 4, 5, 3, 2)).reshape(NB * 4, P, 2048),
        "fox_v": np.ascontiguousarray(a["cache_fox_v"][0].reshape(NB, 4, 2, P, H * HD).transpose(
            0, 1, 3, 2, 4)).reshape(NB * 4, P, 2048),
        "band_k": np.ascontiguousarray(a["cache_band_k"][0].reshape(NB, BW, 4, 2, HD).transpose(
            0, 3, 4, 2, 1)).reshape(NB * 2, P, 2048),
        "band_v": np.ascontiguousarray(a["cache_band_v"][0].reshape(NB, 2, 2, P, H * HD).transpose(
            0, 1, 3, 2, 4)).reshape(NB * 2, P, 2048),
        "rel": np.pad(a["rel_bias"][0][:, ::-1], ((0, 0), (RPAD, 0)), mode="edge"),
        "w_forget": np.ascontiguousarray(w_in[:, f0:f1].reshape(DC, P, H).transpose(1, 0, 2)),
        "b_forget": np.ascontiguousarray(np.broadcast_to(a["b_forget"][0], (P, H))),
        "w_merge": np.stack([np.concatenate([gates[r], branches[r]], axis=1) for r in range(2)]).reshape(
            2 * DC * 3, P, KT * P),
        "w_out": tiles_of(a["w_out"][0]),
        "w_query": tiles_of(a["w_query"][0]),
        "sub_keys": np.ascontiguousarray(a["sub_keys"][0].reshape(2 * H, NKEY, P).transpose(2, 0, 1)),
        "experts": np.concatenate([
            a["expert_u"][0].reshape(P, NGROUP, GROUP, 2, KT, P).transpose(1, 2, 3, 5, 4, 0).reshape(
                NGROUP, 2 * GROUP, P, KT * P),
            a["expert_v"][0].reshape(P, NGROUP, GROUP, DC, P).transpose(1, 3, 0, 2, 4).reshape(
                NGROUP, DC, P, KT * P)], axis=1).reshape(-1, P, KT * P),
    }


def build(nc, inp, proj, logf, y_out):
    negf_p = nc.dram_tensor("negf_prompt", [H, TP], F32, kind="Internal").ap()
    negf_s = nc.dram_tensor("negf_sample", [NB * H, PAST + TS], F32, kind="Internal").ap()
    yt = nc.dram_tensor("mixer_out", [2, H, P, T], F32, kind="Internal").ap()
    gates = nc.dram_tensor("gate_matrix", [NGB, P, NKEY, GB], F32, kind="Internal").ap()
    with ExitStack() as ctx:
        c = Chip(nc, ctx)
        build_constants(c)
        c.end_phase()
        build_ada(c, inp["w_ada"], inp["b_ada"], inp["cond"])
        c.end_phase()
        build_norm(c, "norm_mix", inp["x"], inp["norm_mix"], 1, 0)
        c.end_phase()
        build_projection(c, inp["w_heads"], inp["w_forget"], inp["b_forget"], proj, logf)
        c.end_phase()
        build_forget_sums(c, logf, inp["cache_logf"], negf_p, negf_s)
        c.end_phase()
        build_prompt_attention(c, "fox_prompt", proj, 0, yt[0], negf_p=negf_p)
        c.end_phase()
        build_prompt_attention(c, "band_prompt", proj, 3 * H, yt[1], rel=inp["rel"])
        c.end_phase()
        build_sample_attention(c, "fox_sample", proj, 0, yt[0], PAST, inp["fox_k"], inp["fox_v"],
                               negf_s=negf_s.rearrange("(b h) t -> b h t", h=H))
        c.end_phase()
        build_sample_attention(c, "band_sample", proj, 3 * H, yt[1], BW, inp["band_k"], inp["band_v"], rel=inp["rel"])
        c.end_phase()
        build_merge(c, "merge_fox", inp["w_merge"][0:3 * DC], yt[0], True)
        c.end_phase()
        build_merge(c, "merge_band", inp["w_merge"][3 * DC:6 * DC], yt[1], False)
        c.end_phase()
        build_output(c, inp["w_out"], inp["x"])
        c.end_phase()
        build_norm(c, "norm_ffn", None, inp["norm_ffn"], 4, 3)
        c.end_phase()
        with ExitStack() as found:
            key1_t, key2_t = (c.sb(f"key{i}_t", [P, T], F32, found) for i in (1, 2))
            gate_t = c.sb("gate_t", [P, T], F32, found)
            build_retrieval(c, inp["w_query"], inp["sub_keys"], key1_t, key2_t, gate_t)
            c.end_phase()
            build_gates(c, key1_t, key2_t, gate_t, gates)
            c.end_phase()
        build_experts(c, inp["experts"], gates)
        c.end_phase()
        build_norm(c, "norm_final", None, inp["norm_final"], None, None, out_dram=y_out)
        c.end_phase()


def kernel(**inputs):
    import concourse.bacc as bacc
    from concourse.bass_utils import run_bass_kernel_spmd

    arrays = {f"in_{n}": v for n, v in lay_out({n: np.asarray(v) for n, v in inputs.items()}).items()}
    nc = bacc.Bacc("TRN2", target_bir_lowering=False, num_devices=1)
    inp = {n[3:]: nc.dram_tensor(n, v.shape, mybir.dt.from_np(v.dtype), kind="ExternalInput").ap()
           for n, v in arrays.items()}
    proj = nc.dram_tensor("out_proj", [6 * H, P, T], F32, kind="ExternalOutput").ap()
    logf = nc.dram_tensor("out_logf", [T, H], F32, kind="ExternalOutput").ap()
    y_out = nc.dram_tensor("out_y", [DC, P, T], F32, kind="ExternalOutput").ap()
    build(nc, inp, proj, logf, y_out)
    got = run_bass_kernel_spmd(nc, [arrays], core_ids=[0]).results[0]
    y = got["out_y"].reshape(D, T).T
    tokens = lambda j: got["out_proj"][j * H:(j + 1) * H].transpose(2, 0, 1)
    prompt = lambda j: np.ascontiguousarray(tokens(j)[None, None, :TP])
    sample = lambda j: np.ascontiguousarray(tokens(j)[TP:].reshape(1, NB, TS, H, HD))
    lf = got["out_logf"]
    return (np.ascontiguousarray(y[None, :TP]), np.ascontiguousarray(y[TP:]).reshape(NB, TS, D),
            prompt(1), prompt(2), np.ascontiguousarray(lf[None, None, :TP]), prompt(4), prompt(5),
            sample(1), sample(2), np.ascontiguousarray(lf[TP:]).reshape(1, NB, TS, H), sample(4), sample(5))
```

```python
from contextlib import ExitStack

import numpy as np

import concourse.bass as bass
from concourse import mybir

F32 = mybir.dt.float32
F32R = mybir.dt.float32r
U32 = mybir.dt.uint32
ALU = mybir.AluOpType
ACT = mybir.ActivationFunctionType
AX = mybir.AxisListType

P = 128
D = 2048
DC = D // P
TP = 512
NB, TS = 8, 16
T = TP + NB * TS
TT = T // P
HALF = T // 2
KT = 8
NC9 = 1 + NB
ADA_FIRST = 2 * D // 512
QUAD = 32
H = 8
HD = 128
PAST = 1024
BW = 512
REL = 128
RPAD = 400
QK_SCALE = HD ** -0.5
EPS = 1e-6
NEG = -1e30
LOWEST = -3e38
NKEY = 128
TOPK = 16
GROUP = 8
NGROUP = NKEY // GROUP
GB = 32
NGB = T // GB
MANY_SEMS = 90
RAW, SPLIT = 4, 2


class Chip:

    def __init__(self, nc, ctx):
        self.nc = nc
        self.ctx = ctx
        self.phase_sems = []
        self.passed = nc.alloc_semaphore(name="passed")
        self.act_hi = self.sb("act_hi", [P, DC, T], F32R)
        self.act_lo = self.sb("act_lo", [P, DC, T], F32R)
        self.acc = self.sb("acc", [P, DC, T], F32)
        self.ada = self.sb("ada", [P, 6 * DC, NC9], F32)
        self.ones = self.sb("ones", [P, P], F32)
        self.ident = self.sb("ident", [P, P], F32)
        self.flip = self.sb("flip", [P, P], F32)
        self.causal = self.sb("causal", [P, P], F32)
        self.head_rows = self.sb("head_rows", [H, H, TS], F32)
        self.query_rows = self.sb("query_rows", [TS, H, TS], F32)
        self.iota = self.sb("iota", [P, P], F32)
        self.scores = ctx.enter_context(nc.psum_tensor("scores", [P, 3 * 512], F32))
        rest = ctx.enter_context(nc.psum_tensor("rest", [P, 5 * 512], F32))
        self.bank = [self.scores[:, b * 512:(b + 1) * 512] for b in range(3)]
        self.bank += [rest[:, b * 512:(b + 1) * 512] for b in range(5)]

    def sb(self, name, shape, dt, ctx=None):
        return (ctx or self.ctx).enter_context(self.nc.sbuf_tensor(name, shape, dt))

    def sem(self, name):
        handle = self.nc.alloc_semaphore(name=name)
        self.phase_sems.append(handle)
        return handle

    def end_phase(self, last=False):
        if last:
            self.phase_sems.append(self.passed)
        elif len(self.phase_sems) < MANY_SEMS:
            return
        self.nc.clear_and_free_semaphores(self.phase_sems)
        self.nc.all_engine_barrier()
        self.phase_sems = []

    def halves(self, b):
        return self.bank[b][:, 0:HALF], self.bank[b + 1][:, 0:HALF]


def own_instruction(c, eng):
    eng.sem_inc(c.passed, 1)


def first_then_loop(eng, count, step):
    step(0, True)
    with eng.Fori(1, count) as i:
        step(i, False)


def build_constants(c):
    nc = c.nc
    filled, done = c.sem("const_filled"), c.sem("const_done")
    with nc.Block() as block:
        @block.gpsimd
        def _(pool):
            pool.memset(c.ones[:], 1.0)
            pool.iota(c.iota[:], pattern=[[1, P]], base=0, channel_multiplier=0,
                      allow_small_or_imprecise_dtypes=True)
            pool.memset(c.ident[:], 0.0).then_inc(filled, 1)
            pool.memset(c.flip[:], 0.0).then_inc(filled, 1)
            pool.memset(c.causal[:], 0.0).then_inc(filled, 1)
            pool.memset(c.head_rows[:], 0.0).then_inc(filled, 1)
            pool.memset(c.query_rows[:], 0.0).then_inc(filled, 1)
            pool.wait_ge(filled, 5)
            pool.affine_select(out=c.ident[:], in_=c.ident[:], compare_op=ALU.not_equal, fill=1.0,
                               base=0, pattern=[[-1, P]], channel_multiplier=1)
            pool.affine_select(out=c.flip[:], in_=c.flip[:], compare_op=ALU.not_equal, fill=1.0,
                               base=1 - P, pattern=[[1, P]], channel_multiplier=1)
            pool.affine_select(out=c.causal[:], in_=c.causal[:], compare_op=ALU.is_ge, fill=NEG,
                               base=0, pattern=[[-1, P]], channel_multiplier=1)
            pool.affine_select(out=c.head_rows[:], in_=c.head_rows[:], compare_op=ALU.not_equal,
                               fill=1.0, base=0, pattern=[[1, H], [0, TS]], channel_multiplier=-1)
            pool.affine_select(out=c.query_rows[:], in_=c.query_rows[:], compare_op=ALU.not_equal,
                               fill=1.0, base=0, pattern=[[0, H], [1, TS]],
                               channel_multiplier=-1).then_inc(done, 1)
            pool.wait_ge(done, 1)


def build_ada(c, small, w_ada, b_ada, cond):
    nc = c.nc
    NW = ADA_FIRST
    KQ = DC // RAW
    FB = 512 // P
    with ExitStack() as tmp:
        ring = c.sb("ada_ring", [P, 2 * RAW, KQ, 512], F32, tmp)
        cond_in = c.sb("cond_in", [P, DC, QUAD], F32, tmp)
        cond_act, bias, add_up = small
        rows = [c.sb(f"ada_rows{b}", [P, 512], F32, tmp) for b in range(2)]
        loaded = [c.sem(f"ada_loaded{s}") for s in range(2 * RAW)]
        small_in, cond_ready = c.sem("ada_small_in"), c.sem("ada_cond_ready")
        add_up_ready = c.sem("ada_add_up_ready")
        tile_used, rows_ready = c.sem("ada_tile_used"), c.sem("ada_rows_ready")
        turned, read_out = c.sem("ada_turned"), c.sem("ada_read_out")
        with nc.Block() as block:
            @block.sync
            def _(sp):
                sp.dma_start(cond_in[:], cond).then_inc(small_in, 16)
                sp.dma_start(bias[:], b_ada).then_inc(small_in, 16)

                def load(i, first):
                    for s in range(2 * RAW):
                        if not first:
                            sp.wait_ge(tile_used, i * (2 * RAW) + (s + 1 - 2 * RAW))
                        sp.dma_start(ring[:, s], w_ada[i * (2 * RAW) + s]).then_inc(loaded[s], 16)

                first_then_loop(sp, NW * RAW // (2 * RAW), load)

            @block.scalar
            def _(act):
                act.wait_ge(small_in, 32)
                act.activation(cond_act[:], cond_in[:], ACT.Silu).then_inc(cond_ready, 1)

            @block.tensor
            def _(pe):
                def turn(n, b):
                    pe.wait_ge(rows_ready, n + 1)
                    for f in range(FB):
                        mm = pe.matmul(c.bank[2 + b][:, f * NC9:(f + 1) * NC9], rows[b][:, f * P:(f + 1) * P], add_up[:],
                                       start=True, stop=True)
                    mm.then_inc(turned, 1)

                def blocks(i, first):
                    for b in range(2):
                        n = i * 2 + b
                        if not first:
                            pe.wait_ge(rows_ready, n - 1)
                        for s in range(RAW):
                            pe.wait_ge(loaded[b * RAW + s], i * 16 + 16)
                            for k in range(KQ):
                                mm = pe.matmul(c.bank[b][k * QUAD:(k + 1) * QUAD, :], cond_act[:, s * KQ + k, :],
                                               ring[:, b * RAW + s, k, :], start=(s == 0), stop=(s == RAW - 1),
                                               skip_group_check=True)
                            mm.then_inc(tile_used, 1)
                        if not (first and b == 0):
                            if not (first and b == 1):
                                pe.wait_ge(read_out, n - 2)
                            turn(n - 1, (b + 1) % 2)

                pe.wait_ge(cond_ready, 1)
                pe.wait_ge(add_up_ready, 1)
                first_then_loop(pe, NW // 2, blocks)
                turn(NW - 1, 1)

            @block.vector
            def _(dve):
                def evacuate(i, first):
                    for b in range(2):
                        n = i * 2 + b
                        dve.wait_ge(tile_used, n * RAW + RAW)
                        if not first:
                            dve.wait_ge(turned, n - 1)
                        dve.tensor_copy(rows[b][:], c.bank[b][:]).then_inc(rows_ready, 1)
                        if not (first and b == 0):
                            finish(n - 1, (b + 1) % 2)

                def finish(n, b):
                    dve.wait_ge(turned, n + 1)
                    dve.tensor_tensor(c.ada[:, bass.ds(n * FB, FB), :],
                                      c.bank[2 + b][:, 0:FB * NC9].rearrange("p (f c) -> p f c", c=NC9),
                                      bias[:, bass.ds(n * FB, FB)].unsqueeze(2).broadcast_to([P, FB, NC9]),
                                      ALU.add).then_inc(read_out, 1)

                dve.tensor_reduce(add_up[:], c.ident[:].rearrange("p (g c) -> p c g", c=QUAD)[:, 0:NC9, :], AX.X,
                                  ALU.add).then_inc(add_up_ready, 1)
                dve.wait_ge(small_in, 32)
                first_then_loop(dve, NW // 2, evacuate)
                finish(NW - 1, 1)


class LateAda:

    def __init__(self, c, tmp, small, w_ada):
        self.c, self.w_ada = c, w_ada
        self.cond_act, self.bias, self.add_up = small
        self.ring = c.sb("late_ada_ring", [P, RAW, DC // RAW, 512], F32, tmp)
        self.rows = [c.sb(f"late_ada_rows{e}", [P, 512], F32, tmp) for e in range(2)]
        self.loaded = [c.sem(f"late_ada_loaded{s}") for s in range(RAW)]
        self.used, self.rows_ready, self.turned, self.added = (
            c.sem(f"late_ada_{n}") for n in ("used", "rows_ready", "turned", "added"))

    def load(self, eng, i, e, pair):
        for s in (2 * pair, 2 * pair + 1):
            if not (isinstance(i, int) and i == 0 and e == 0):
                eng.wait_ge(self.used, (i * 2 + (e - 1)) * RAW + (s + 1))
            eng.dma_start(self.ring[:, s], self.w_ada[(i * 2 + (e + ADA_FIRST)) * RAW + s]).then_inc(self.loaded[s], 16)

    def multiply(self, pe, i, e, pair):
        for s in (2 * pair, 2 * pair + 1):
            pe.wait_ge(self.loaded[s], (i * 2 + e) * 16 + 16)
            for k in range(DC // RAW):
                mm = pe.matmul(self.c.bank[4 + e][k * QUAD:(k + 1) * QUAD, :], self.cond_act[:, s * RAW + k, :],
                               self.ring[:, s, k, :], start=(s == 0), stop=(s == RAW - 1), skip_group_check=True)
            mm.then_inc(self.used, 1)

    def copy(self, dve, i, e):
        dve.wait_ge(self.used, (i * 2 + e) * RAW + RAW)
        dve.tensor_copy(self.rows[e][:], self.c.bank[4 + e][:]).then_inc(self.rows_ready, 1)

    def turn(self, pe, i, e):
        pe.wait_ge(self.rows_ready, i * 2 + (e + 1))
        pe.wait_ge(self.added, i * 2 + (e + 1))
        for f in range(512 // P):
            mm = pe.matmul(self.c.bank[6 + e][:, f * NC9:(f + 1) * NC9], self.rows[e][:, f * P:(f + 1) * P], self.add_up[:],
                           start=True, stop=True)
        mm.then_inc(self.turned, 1)

    def add(self, dve, i, e):
        dve.wait_ge(self.turned, i * 2 + (e + 1))
        fb = 512 // P
        at = bass.ds((i * 2 + (e + ADA_FIRST)) * fb, fb)
        dve.tensor_tensor(self.c.ada[:, at, :], self.c.bank[6 + e][:, 0:fb * NC9].rearrange("p (f c) -> p f c", c=NC9),
                          self.bias[:, at].unsqueeze(2).broadcast_to([P, fb, NC9]), ALU.add).then_inc(self.added, 1)


def build_norm(c, name, x_dram, gain, scale_row, shift_row, out_dram=None):
    nc = c.nc
    NBF = 4
    with ExitStack() as tmp:
        gains = c.sb(f"{name}_gains", [P, DC], F32, tmp)
        square = c.sb(f"{name}_square", [P, 2, T], F32, tmp)
        rstd = c.sb(f"{name}_rstd", [P, T], F32, tmp)
        normed = c.sb(f"{name}_normed", [P, NBF, T], F32, tmp)
        value = c.sb(f"{name}_value", [P, NBF, T], F32, tmp)
        mult = c.sb(f"{name}_mult", [P, DC, NC9], F32, tmp)
        sem = {n: c.sem(f"{name}_{n}") for n in
               ("gain_in", "squared", "summed", "sum_done", "var", "root", "rstd_ready", "mult_ready",
                "normed", "affine", "sample_a", "sample", "hi", "lo", "out_used")}
        x_in = [c.sem(f"{name}_x_in{q}") for q in range(4)]
        stored = [c.sem(f"{name}_stored{b}") for b in range(NBF)]
        sums = c.halves(0)
        with nc.Block() as block:
            @block.sync
            def _(sp):
                sp.dma_start(gains[:], gain).then_inc(sem["gain_in"], 16)
                if x_dram is not None:
                    for q in range(4):
                        sp.dma_start(c.acc[:, 4 * q:4 * q + 4, :],
                                     x_dram[4 * q:4 * q + 4].rearrange("k p t -> p k t")).then_inc(x_in[q], 16)
                if out_dram is not None:
                    with sp.Fori(0, DC // NBF) as i:
                        for b in range(NBF):
                            sp.wait_ge(sem["normed"], i * NBF + (b + 1))
                            sp.dma_start(out_dram[i * NBF + b], value[:, b, :]).then_inc(stored[b], 16)
                    for b in range(NBF):
                        sp.wait_ge(stored[b], 16 * (DC // NBF))

            @block.scalar
            def _(act):
                for k in range(DC):
                    if x_dram is not None and k % 4 == 0:
                        act.wait_ge(x_in[k // 4], 16)
                    if k >= 2:
                        act.wait_ge(sem["summed"], k - 1)
                    act.activation(square[:, k % 2, :], c.acc[:, k, :], ACT.Square).then_inc(sem["squared"], 1)
                act.wait_ge(sem["var"], 2)
                act.activation(rstd[:], rstd[:], ACT.Sqrt).then_inc(sem["root"], 1)
                if out_dram is None:
                    act.wait_ge(sem["mult_ready"], 1)
                    with act.Fori(0, DC // NBF) as i:
                        for b in range(NBF):
                            k = i * NBF + b
                            act.wait_ge(sem["normed"], k + 1)
                            act.wait_ge(sem["lo"], k + 1)
                            act.activation(value[:, b, 0:TP], normed[:, b, 0:TP], ACT.Identity,
                                           scale=mult[:, k, 0:1],
                                           bias=c.ada[:, k + shift_row * DC, 0:1]).then_inc(sem["affine"], 1)
                            act.wait_ge(sem["affine"], k + 1)
                            act.wait_ge(sem["sample"], k + 1)
                            act.activation(c.act_hi[:, k, :], value[:, b, :], ACT.Copy).then_inc(sem["hi"], 1)

            @block.tensor
            def _(pe):
                for k in range(DC):
                    pe.wait_ge(sem["squared"], k + 1)
                    for h in range(2):
                        mm = pe.matmul(sums[h], c.ones[:], square[:, k % 2, h * HALF:(h + 1) * HALF],
                                       start=(k == 0), stop=(k == DC - 1))
                    mm.then_inc(sem["summed"], 1)

            @block.vector
            def _(dve):
                dve.wait_ge(sem["gain_in"], 16)
                if out_dram is None:
                    dve.scalar_tensor_tensor(out=mult[:], in0=c.ada[:, scale_row * DC:(scale_row + 1) * DC, :],
                                             scalar=1.0,
                                             in1=gains[:].unsqueeze(2).broadcast_to([P, DC, NC9]),
                                             op0=ALU.add, op1=ALU.mult).then_inc(sem["mult_ready"], 1)
                dve.wait_ge(sem["summed"], DC)
                for h in range(2):
                    dve.tensor_scalar(rstd[:, h * HALF:(h + 1) * HALF], sums[h], 1.0 / D, EPS,
                                      ALU.mult, ALU.add).then_inc(sem["var"], 1)
                dve.wait_ge(sem["root"], 1)
                dve.reciprocal(rstd[:], rstd[:]).then_inc(sem["rstd_ready"], 1)
                dve.wait_ge(sem["rstd_ready"], 1)
                if out_dram is not None:
                    for k in range(DC):
                        if k >= NBF:
                            dve.wait_ge(stored[k % NBF], 16 * (k // NBF))
                        dve.scalar_tensor_tensor(out=value[:, k % NBF, :], in0=c.acc[:, k, :],
                                                 scalar=gains[:, k:k + 1], in1=rstd[:],
                                                 op0=ALU.mult, op1=ALU.mult).then_inc(sem["normed"], 1)
                    return
                dve.wait_ge(sem["mult_ready"], 1)
                dve.sem_inc(sem["lo"], NBF)

                with dve.Fori(0, DC // NBF) as i:
                    for b in range(NBF):
                        k = i * NBF + b
                        row = normed[:, b, TP:T].rearrange("p (s t) -> p s t", s=NB)
                        val = value[:, b, TP:T].rearrange("p (s t) -> p s t", s=NB)
                        dve.wait_ge(sem["lo"], k + 1)
                        dve.tensor_tensor(normed[:, b, :], c.acc[:, k, :], rstd[:], ALU.mult).then_inc(sem["normed"], 1)
                        dve.wait_ge(sem["normed"], k + 1)
                        dve.tensor_tensor(val, row, mult[:, k, 1:NC9].unsqueeze(2).broadcast_to([P, NB, TS]),
                                          ALU.mult).then_inc(sem["sample_a"], 1)
                        dve.wait_ge(sem["sample_a"], k + 1)
                        dve.tensor_tensor(val, val, c.ada[:, k + shift_row * DC, 1:NC9].unsqueeze(2).broadcast_to([P, NB, TS]),
                                          ALU.add).then_inc(sem["sample"], 1)

            if out_dram is None:
                @block.gpsimd
                def _(pool):
                    with pool.Fori(0, DC // NBF) as i:
                        for b in range(NBF):
                            k = i * NBF + b
                            pool.wait_ge(sem["hi"], k + 1)
                            own_instruction(c, pool)
                            pool.tensor_tensor(c.act_lo[:, k, :], value[:, b, :], c.act_hi[:, k, :].bitcast(F32),
                                               ALU.subtract).then_inc(sem["lo"], 1)


class WeightStream:

    def __init__(self, c, tmp, name):
        self.c = c
        self.raw = c.sb(f"{name}_raw", [P, RAW, KT * P], F32, tmp)
        self.hi = [c.sb(f"{name}_w_hi{s}", [P, KT * P], F32R, tmp) for s in range(SPLIT)]
        self.lo = [c.sb(f"{name}_w_lo{s}", [P, KT * P], F32R, tmp) for s in range(SPLIT)]
        self.loaded = [c.sem(f"{name}_loaded{s}") for s in range(RAW)]
        self.rounded = c.sem(f"{name}_rounded")
        self.split = c.sem(f"{name}_split")
        self.used = c.sem(f"{name}_used")

    def load_four(self, sp, tiles, n, count=RAW):
        for s in range(count):
            sp.wait_ge(self.split, n + (s + 1))
            sp.dma_start(self.raw[:, s], tiles[n + s]).then_inc(self.loaded[s], 16)

    def load(self, sp, tiles, count):
        with sp.Fori(0, count // RAW) as i:
            self.load_four(sp, tiles, i * RAW)
        if count % RAW:
            self.load_four(sp, tiles, count // RAW * RAW, count % RAW)

    def divide(self, pool, count):
        pool.sem_inc(self.split, RAW)
        pool.sem_inc(self.used, SPLIT)

        def four(i, slots):
            for s in range(slots):
                n = i * RAW + s
                pool.wait_ge(self.loaded[s], i * 16 + 16)
                pool.wait_ge(self.used, n + 1)
                own_instruction(self.c, pool)
                pool.tensor_tensor(self.hi[s % SPLIT][:].rearrange("p (k n) -> p k n", k=KT),
                                   self.raw[:, s].rearrange("p (k n) -> p k n", k=KT),
                                   self.c.ones[:, 0:1].unsqueeze(2).broadcast_to([P, KT, P]),
                                   ALU.mult).then_inc(self.rounded, 1)
                pool.wait_ge(self.rounded, n + 1)
                pool.tensor_tensor(self.lo[s % SPLIT][:], self.raw[:, s],
                                   self.hi[s % SPLIT][:].bitcast(F32), ALU.subtract).then_inc(self.split, 1)

        with pool.Fori(0, count // RAW) as i:
            four(i, RAW)
        four(count // RAW, count % RAW)

    def multiply(self, pe, n, slot, out, x_hi, x_lo, k0, start, stop, chunk_ready=None, ready_from=0):
        pe.wait_ge(self.split, n + (1 + RAW))
        for k in range(KT):
            if chunk_ready is not None:
                pe.wait_ge(chunk_ready, ready_from + (k0 + k + 1))
            hi, lo = (w[slot][:, k * P:(k + 1) * P] for w in (self.hi, self.lo))
            for j, (w, x) in enumerate(((hi, x_hi), (hi, x_lo), (lo, x_hi))):
                for h in range(2):
                    mm = pe.matmul(out[h], w, x[:, k0 + k, h * HALF:(h + 1) * HALF],
                                   start=(start and k == 0 and j == 0), stop=(stop and k == KT - 1 and j == 2))
        mm.then_inc(self.used, 1)


def build_projection(c, w_heads, b_forget, proj, logf, ada_small, w_ada):
    nc = c.nc
    NM = 6 * H
    PER = 6
    ROUNDS = NM // PER
    with ExitStack() as tmp:
        ws = WeightStream(c, tmp, "proj")
        late = LateAda(c, tmp, ada_small, w_ada)
        stage = c.sb("proj_stage", [P, 2, T], F32, tmp)
        z_rows = c.sb("forget_rows", [H, T], F32, tmp)
        fb = c.sb("forget_b", [P, H], F32, tmp)
        z, e, lg, mn = (c.sb(f"forget_{n}", [P, TT, H], F32, tmp) for n in ("z", "e", "log", "min"))
        small_in, z_ready = c.sem("proj_small_in"), c.sem("forget_rows_ready")
        half0, half1 = c.sem("proj_half0"), c.sem("proj_half1")
        stored = [c.sem(f"proj_stored{b}") for b in range(2)]
        forget, fstep, fact, fstored = c.sem("forget_product"), c.sem("forget_step"), c.sem("forget_act"), c.sem("forget_stored")
        out = [c.halves(0), c.halves(2)]
        with nc.Block() as block:
            @block.sync
            def _(sp):
                sp.dma_start(fb[:], b_forget).then_inc(small_in, 16)
                ws.load(sp, w_heads, 2 * (NM + 1))
                sp.wait_ge(fstep, 5)
                sp.dma_start(logf.rearrange("(t p) h -> p t h", p=P), lg[:]).then_inc(fstored, 16)
                sp.wait_ge(fstored, 16)

            @block.gpsimd
            def _(pool):
                ws.divide(pool, 2 * (NM + 1))

            @block.tensor
            def _(pe):
                for kh in range(2):
                    ws.multiply(pe, kh, kh, c.halves(4), c.act_hi, c.act_lo, kh * KT, kh == 0, kh == 1)
                pe.wait_ge(z_ready, 1)
                for t in range(TT):
                    mm = pe.transpose(c.bank[6][:, t * H:(t + 1) * H], z_rows[:, t * P:(t + 1) * P], c.ident[0:H, 0:H])
                mm.then_inc(forget, 1)
                with pe.Fori(0, ROUNDS) as i:
                    for q in range(PER):
                        m = i * PER + q
                        pe.wait_ge(half0, m + 1)
                        pe.wait_ge(half1, m + 1)
                        for kh in range(2):
                            ws.multiply(pe, m * 2 + (2 + kh), kh, out[q % 2], c.act_hi, c.act_lo, kh * KT, kh == 0, kh == 1)
                        if q % 3 < 2:
                            late.multiply(pe, i, q // 3, q % 3)
                        else:
                            late.turn(pe, i, q // 3)

            @block.scalar
            def _(act):
                for pair in range(2):
                    late.load(act, 0, 0, pair)
                act.sem_inc(half0, 2)
                act.wait_ge(fstep, 4)
                act.activation(e[:], e[:], ACT.Exp).then_inc(fact, 1)
                act.wait_ge(fact, 1)
                act.activation(lg[:], e[:], ACT.Ln, bias=1.0).then_inc(fact, 1)

                def evacuate(i, first, last=False):
                    for q in range(PER):
                        m, b = i * PER + q, q % 2
                        act.wait_ge(ws.used, m * 2 + (4 + SPLIT))
                        if not (first and q < 2):
                            act.wait_ge(stored[b], (i * (PER // 2) + q // 2) * 16)
                        act.activation(stage[:, b, 0:HALF], out[b][0], ACT.Copy).then_inc(half0, 1)
                        act.wait_ge(half0, m + 3)
                        act.wait_ge(half1, m + 3)
                        act.dma_start(proj[m], stage[:, b, :]).then_inc(stored[b], 16)
                        if q in (1, 2):
                            late.load(act, i, 1, q - 1)
                        elif q in (4, 5) and not last:
                            late.load(act, i + 1, 0, q - 4)

                evacuate(0, True)
                with act.Fori(1, ROUNDS - 1) as i:
                    evacuate(i, False)
                evacuate(ROUNDS - 1, False, last=True)
                for b in range(2):
                    act.wait_ge(stored[b], 16 * (NM // 2))

            @block.vector
            def _(dve):
                dve.sem_inc(half1, 2)
                dve.sem_inc(late.added, 2)
                dve.wait_ge(ws.used, 2 + SPLIT)
                for j in range(2):
                    op = dve.tensor_copy(z_rows[:, j * HALF:(j + 1) * HALF], c.halves(4)[j][0:H, :])
                op.then_inc(z_ready, 1)
                dve.wait_ge(small_in, 16)
                dve.wait_ge(forget, 1)
                dve.tensor_tensor(z[:], c.bank[6][:, 0:TT * H].rearrange("p (t h) -> p t h", h=H),
                                  fb[:].unsqueeze(1).broadcast_to([P, TT, H]), ALU.add).then_inc(fstep, 1)
                dve.wait_ge(fstep, 1)
                dve.tensor_scalar(mn[:], z[:], 0.0, None, ALU.min).then_inc(fstep, 1)
                dve.tensor_scalar(e[:], z[:], 0.0, None, ALU.max).then_inc(fstep, 1)
                dve.wait_ge(fstep, 3)
                dve.tensor_tensor(e[:], mn[:], e[:], ALU.subtract).then_inc(fstep, 1)
                dve.wait_ge(fact, 2)
                dve.tensor_tensor(lg[:], mn[:], lg[:], ALU.subtract).then_inc(fstep, 1)

                def evacuate(i, first):
                    for q in range(PER):
                        b = q % 2
                        dve.wait_ge(ws.used, (i * PER + q) * 2 + (4 + SPLIT))
                        if not (first and q < 2):
                            dve.wait_ge(stored[b], (i * (PER // 2) + q // 2) * 16)
                        dve.tensor_copy(stage[:, b, HALF:T], out[b][1]).then_inc(half1, 1)
                        if q % 3 == 1:
                            late.copy(dve, i, q // 3)
                        elif q % 3 == 2:
                            late.add(dve, i, q // 3)

                first_then_loop(dve, ROUNDS, evacuate)


def build_forget_sums(c, logf, cache_logf, negf_p, negf_s):
    nc = c.nc
    NK = PAST // P
    with ExitStack() as tmp:
        triangle = c.sb("triangle", [P, P + PAST], F32, tmp)
        lp = c.sb("logf_prompt", [P, TP // P, H], F32, tmp)
        ls = c.sb("logf_past", [P, NK, NB * H], F32, tmp)
        ln = c.sb("logf_new", [TS, NB, H], F32, tmp)
        out_p = c.sb("negf_p_sb", [H, TP], F32, tmp)
        out_s = c.sb("negf_s_sb", [NB * H, PAST + TS], F32, tmp)
        small_in, filled, made = c.sem("logf_in"), c.sem("triangle_filled"), c.sem("triangle_made")
        summed, copied, stored = c.sem("forget_summed"), c.sem("negf_copied"), c.sem("negf_stored")
        with nc.Block() as block:
            @block.gpsimd
            def _(pool):
                pool.memset(triangle[:], -1.0).then_inc(filled, 1)
                pool.wait_ge(filled, 1)
                pool.affine_select(out=triangle[:], in_=triangle[:], compare_op=ALU.is_ge, fill=0.0, base=0,
                                   pattern=[[1, P + PAST]], channel_multiplier=-1).then_inc(made, 1)

            @block.sync
            def _(sp):
                sp.dma_start(lp[:], logf[0:TP].rearrange("(t p) h -> p t h", p=P)).then_inc(small_in, 16)
                sp.dma_start(ls[:], cache_logf).then_inc(small_in, 16)
                sp.dma_start(ln[:], logf[TP:T].rearrange("(b i) h -> i b h", i=TS)).then_inc(small_in, 16)
                sp.wait_ge(copied, 2)
                sp.dma_start(negf_p, out_p[:]).then_inc(stored, 16)
                sp.dma_start(negf_s, out_s[:]).then_inc(stored, 16)
                sp.wait_ge(stored, 32)

            @block.tensor
            def _(pe):
                pe.wait_ge(small_in, 48)
                pe.wait_ge(made, 1)
                for k in reversed(range(TP // P)):
                    mm = pe.matmul(c.bank[3][0:H, k * P:TP], lp[:, k, :], triangle[:, 0:TP - k * P],
                                   start=(k == TP // P - 1), stop=(k == 0), skip_group_check=True)
                mm.then_inc(summed, 1)
                pe.matmul(c.bank[2][0:NB * H, 0:TS], ln[:].rearrange("i b h -> i (b h)"), triangle[0:TS, 0:TS],
                          start=True, stop=False, skip_group_check=True)
                for k in reversed(range(NK)):
                    for b, end in enumerate((512, 1024, PAST + TS)):
                        at = max(k * P, b * 512)
                        if at < end:
                            mm = pe.matmul(c.bank[b][0:NB * H, at - b * 512:end - b * 512], ls[:, k, :],
                                           triangle[:, at - k * P:end - k * P],
                                           start=(b < 2 and k == 4 * b + 3), stop=(k == 0), skip_group_check=True)
                mm.then_inc(summed, 1)

            @block.vector
            def _(dve):
                dve.wait_ge(summed, 1)
                dve.tensor_copy(out_p[:], c.bank[3][0:H, :]).then_inc(copied, 1)
                dve.wait_ge(summed, 2)
                for b in range(2):
                    dve.tensor_copy(out_s[:, b * 512:(b + 1) * 512], c.bank[b][0:NB * H, :])
                dve.tensor_copy(out_s[:, PAST:PAST + TS], c.bank[2][0:NB * H, 0:TS]).then_inc(copied, 1)


def build_prompt_attention(c, name, proj, base, yt, negf_p=None, rel=None):
    nc = c.nc
    NQ = TP // P
    with ExitStack() as tmp:
        qkv = c.sb(f"{name}_qkv", [P, 2, 3, TP], F32, tmp)
        q = c.sb(f"{name}_q", [P, 2, TP], F32, tmp)
        v = c.sb(f"{name}_v", [P, NQ, P], F32, tmp)
        prob = c.sb(f"{name}_prob", [P, NQ, TP], F32, tmp)
        prob_t = c.sb(f"{name}_prob_t", [P, NQ, TP], F32, tmp)
        stat = c.sb(f"{name}_stat", [P, 3, NQ], F32, tmp)
        y = c.sb(f"{name}_y", [P, 2, TP], F32, tmp)
        if rel is None:
            bias = c.sb(f"{name}_bias", [1, H * TP], F32, tmp)
        else:
            bias = c.sb(f"{name}_bias", [P, H, TP], F32, tmp)
        sem = {n: c.sem(f"{name}_{n}") for n in
               ("bias_in", "bias_ready", "q", "v_turned", "v", "scores", "maxed", "exped", "recip", "prob",
                "turned", "prob_t", "y_product", "y")}
        loaded = [c.sem(f"{name}_loaded{b}") for b in range(2)]
        stored = [c.sem(f"{name}_stored{b}") for b in range(2)]
        with nc.Block() as block:
            @block.sync
            def _(sp):
                if rel is None:
                    sp.dma_start(bias[:], negf_p.rearrange("h t -> (h t)").unsqueeze(0)).then_inc(sem["bias_in"], 16)
                else:
                    row = rel.shape[1]
                    sp.dma_start(bias[:], bass.AP(tensor=rel.tensor, offset=rel.offset + RPAD - (TP - P - REL) - (P - 1),
                                                  ap=[[1, P], [row, H], [1, TP]])).then_inc(sem["bias_in"], 16)

                def load(i, first):
                    for b in range(2):
                        if not first:
                            sp.wait_ge(sem["turned"], (i * 2 + (b - 2)) * NQ + NQ)
                        for j in range(3):
                            sp.dma_start(qkv[:, b, j], proj[i * 2 + (base + j * H + b), :, 0:TP]).then_inc(loaded[b], 16)

                first_then_loop(sp, H // 2, load)

            if rel is not None:
                @block.gpsimd
                def _(pool):
                    pool.wait_ge(sem["bias_in"], 16)
                    pool.memset(bias[P // 2:P, :, TP - P // 2:TP], NEG).then_inc(sem["bias_ready"], 1)

            @block.tensor
            def _(pe):
                if rel is None:
                    pe.wait_ge(sem["bias_in"], 16)
                else:
                    pe.wait_ge(sem["bias_ready"], 1)

                def head(i, first):
                    for b in range(2):
                        h = i * 2 + b
                        pe.wait_ge(loaded[b], i * 48 + 48)
                        pe.wait_ge(sem["q"], h + 1)
                        for t in range(NQ):
                            n = (t + 1) * P
                            if not (first and b == 0):
                                pe.wait_ge(sem["exped"], (h - 1) * NQ + (t + 1))
                            out = c.bank[t][:, 0:n]
                            if rel is None:
                                pe.matmul(c.bank[t][:, t * P:n], c.ident[:], c.causal[:], start=True, stop=False,
                                          skip_group_check=True)
                            pe.matmul(out, q[:, b, t * P:(t + 1) * P], qkv[:, b, 1, 0:n], start=(rel is not None), stop=False,
                                      skip_group_check=True)
                            if rel is None:
                                mm = pe.matmul(out, c.ones[0:1, :], bias[0:1, bass.ds(h * TP, n)], start=False, stop=True,
                                               skip_group_check=True)
                            else:
                                mm = pe.matmul(out, c.flip[:], bias[:, h, TP - n:TP], start=False, stop=True, skip_group_check=True)
                            mm.then_inc(sem["scores"], 1)
                        if not (first and b == 0):
                            values(h - 1, not (first and b == 1))
                        for k in range(NQ):
                            mm = pe.transpose(c.bank[4][:, k * P:(k + 1) * P], qkv[:, b, 2, k * P:(k + 1) * P], c.ident[:])
                        mm.then_inc(sem["v_turned"], 1)
                        for t in range(NQ):
                            r = h * NQ + t
                            pe.wait_ge(sem["prob"], r + 1)
                            if not (first and b == 0 and t < 2):
                                pe.wait_ge(sem["prob_t"], r - 1)
                            for k in range(t + 1):
                                mm = pe.transpose(c.bank[5 + t % 2][:, k * P:(k + 1) * P], prob[:, t, k * P:(k + 1) * P], c.ident[:])
                            mm.then_inc(sem["turned"], 1)

                def values(h, used):
                    pe.wait_ge(sem["prob_t"], h * NQ + NQ)
                    pe.wait_ge(sem["v"], h + 1)
                    if used:
                        pe.wait_ge(sem["y"], h)
                    for k in reversed(range(NQ)):
                        mm = pe.matmul(c.bank[7][:, k * P:TP], v[:, k, :], prob_t[:, k, k * P:TP],
                                       start=(k == NQ - 1), stop=(k == 0), skip_group_check=True)
                    mm.then_inc(sem["y_product"], 1)

                first_then_loop(pe, H // 2, head)
                values(H - 1, True)

            @block.scalar
            def _(act):
                def head(i, first):
                    for b in range(2):
                        h = i * 2 + b
                        for t in range(NQ):
                            r = h * NQ + t
                            act.wait_ge(sem["maxed"], r + 1)
                            if not (first and b == 0):
                                act.wait_ge(sem["turned"], r - (NQ - 1))
                            act.activation(prob[:, t, 0:(t + 1) * P], c.bank[t][:, 0:(t + 1) * P], ACT.Exp,
                                           bias=stat[:, 0, t:t + 1], accum_out=stat[:, 1, t:t + 1]).then_inc(sem["exped"], 1)
                        act.wait_ge(sem["v_turned"], h + 1)
                        act.activation(v[:], c.bank[4][:].rearrange("p (k d) -> p k d", d=P), ACT.Copy).then_inc(sem["v"], 1)
                        for t in range(NQ):
                            act.wait_ge(sem["turned"], h * NQ + (t + 1))
                            act.activation(prob_t[:, 0:t + 1, t * P:(t + 1) * P],
                                           c.bank[5 + t % 2][:, 0:(t + 1) * P].rearrange("p (k q) -> p k q", q=P),
                                           ACT.Copy).then_inc(sem["prob_t"], 1)

                first_then_loop(act, H // 2, head)

            @block.vector
            def _(dve):
                def head(i, first):
                    for b in range(2):
                        h = i * 2 + b
                        dve.wait_ge(loaded[b], i * 48 + 48)
                        dve.tensor_scalar(q[:, b], qkv[:, b, 0], QK_SCALE, None, ALU.mult).then_inc(sem["q"], 1)
                        for t in range(NQ):
                            dve.wait_ge(sem["scores"], h * NQ + (t + 1))
                            dve.tensor_reduce(stat[:, 0, t:t + 1], c.bank[t][:, 0:(t + 1) * P], AX.X, ALU.max,
                                              negate=True).then_inc(sem["maxed"], 1)
                        for t in range(NQ):
                            r = h * NQ + t
                            dve.wait_ge(sem["exped"], r + 1)
                            dve.reciprocal(stat[:, 2, t:t + 1], stat[:, 1, t:t + 1]).then_inc(sem["recip"], 1)
                            dve.wait_ge(sem["recip"], r + 1)
                            dve.tensor_scalar(prob[:, t, 0:(t + 1) * P], prob[:, t, 0:(t + 1) * P], stat[:, 2, t:t + 1],
                                              None, ALU.mult).then_inc(sem["prob"], 1)
                        if b == 1:
                            keep(h - 1, 0, i)
                        elif not first:
                            keep(h - 1, 1, i - 1)

                def keep(h, b, stores):
                    dve.wait_ge(sem["y_product"], h + 1)
                    if not (isinstance(stores, int) and stores == 0):
                        dve.wait_ge(stored[b], stores * 16)
                    dve.tensor_copy(y[:, b], c.bank[7][:]).then_inc(sem["y"], 1)

                head(0, True)
                head(1, False)
                with dve.Fori(2, H // 2) as i:
                    head(i, False)
                keep(H - 1, 1, H // 2 - 1)

            @block.gpsimd
            def _(pool):
                with pool.Fori(0, H // 2) as i:
                    for b in range(2):
                        pool.wait_ge(sem["y"], i * 2 + (b + 1))
                        pool.dma_start(yt[i * 2 + b, :, 0:TP], y[:, b]).then_inc(stored[b], 16)
                for b in range(2):
                    pool.wait_ge(stored[b], 16 * (H // 2))


def build_sample_attention(c, name, proj, base, yt, past, k_cache, v_cache, negf_s=None, rel=None):
    nc = c.nc
    L = past + TS
    NK = past // P
    NT = H * past // 2048
    PAIRS = H // 2
    PW = 2 * TS
    KV = NK // NT
    NBK = past // 512
    with ExitStack() as tmp:
        k_ring = c.sb(f"{name}_k_ring", [P, NT, PAIRS, 512], F32, tmp)
        v_ring = c.acc[:].rearrange("p k t -> p (k t)")[:, 0:NT * 2048].rearrange(
            "p (s b n) -> p s b n", s=NT, b=KV)
        new = c.sb(f"{name}_new", [P, 3, H, P], F32, tmp)
        q_pad = c.sb(f"{name}_q_pad", [P, H, P + TS], F32, tmp)
        k_new = c.sb(f"{name}_k_new", [P, H, TS], F32, tmp)
        v_new = c.sb(f"{name}_v_new", [P, H, TS], F32, tmp)
        v_rows = c.sb(f"{name}_v_rows", [TS, H * HD], F32, tmp)
        prob = c.sb(f"{name}_prob", [P, L], F32, tmp)
        prob_t = c.sb(f"{name}_prob_t", [P, NK + 1, P], F32, tmp)
        stat = c.sb(f"{name}_stat", [P, 3], F32, tmp)
        o_rows = c.sb(f"{name}_o_rows", [P, 2 * HD], F32, tmp)
        y = c.sb(f"{name}_y", [P, H, P], F32, tmp)
        if rel is None:
            bias = c.sb(f"{name}_bias", [H, L], F32, tmp)
        else:
            bias = c.sb(f"{name}_bias", [P, L], F32, tmp)
        sem = {n: c.sem(f"{name}_{n}") for n in
               ("new_in", "bias_in", "zeroed", "picked", "k_used", "v_used", "v_turned", "v_rows", "v_rows_used", "scores", "maxed",
                "exped", "recip", "prob", "turned", "prob_t", "o_rows", "o_turned", "y", "stored")}
        k_in = [c.sem(f"{name}_k_in{s}") for s in range(NT)]
        v_in = [c.sem(f"{name}_v_in{s}") for s in range(NT)]
        q_flat = q_pad[:].rearrange("p h n -> p (h n)")
        s_bank = lambda j: c.bank[j]
        with nc.Block() as block:
            @block.sync
            def _(sp):
                for j in range(3):
                    sp.dma_start(new[:, j], proj[base + j * H:base + (j + 1) * H, :, TP:T].rearrange(
                        "h p t -> p h t")).then_inc(sem["new_in"], 16)
                if rel is not None:
                    row = rel.shape[1]
                    for h in range(H):
                        sp.dma_start(bias[(H - 1 - h) * TS:(H - h) * TS, :],
                                     bass.AP(tensor=rel.tensor, offset=rel.offset + h * row + RPAD - (past - REL) - (TS - 1),
                                             ap=[[1, TS], [1, L]])).then_inc(sem["bias_in"], 16)

                def load_keys(b, first):
                    if rel is None:
                        if not first:
                            sp.wait_ge(sem["scores"], b)
                        sp.dma_start(bias[:], negf_s[b]).then_inc(sem["bias_in"], 16)
                    for s in range(NT):
                        if not first:
                            sp.wait_ge(sem["k_used"], b * NT + (s + 1 - NT))
                        sp.dma_start(k_ring[:, s].rearrange("p h n -> p (h n)"), k_cache[b * NT + s]).then_inc(k_in[s], 16)

                def load_values(b, first):
                    for s in range(NT):
                        if not first:
                            sp.wait_ge(sem["v_used"], b * NT + (s + 1 - NT))
                        sp.dma_start(v_ring[:, s].rearrange("p b n -> p (b n)"), v_cache[b * NT + s]).then_inc(v_in[s], 16)

                load_keys(0, True)
                load_keys(1, False)
                load_values(0, True)
                with sp.Fori(2, NB) as b:
                    load_keys(b, False)
                    load_values(b - 1, False)
                load_values(NB - 1, False)
                sp.wait_ge(sem["y"], NB)
                sp.dma_start(yt[:, :, TP:T].rearrange("h p t -> p h t"), y[:]).then_inc(sem["stored"], 16)
                sp.wait_ge(sem["stored"], 16)

            @block.gpsimd
            def _(pool):
                pool.memset(q_pad[:], 0.0).then_inc(sem["zeroed"], 1)

            @block.tensor
            def _(pe):
                if rel is not None:
                    pe.wait_ge(sem["bias_in"], 16 * H)

                def sequence(b, first):
                    pe.wait_ge(sem["picked"], b * 3 + 3)
                    def stationary(h):
                        return q_flat[:, h * P + h // 2 * PW:h * P + (h // 2 + 1) * PW]

                    for odd in range(2):
                        for g in range(PAIRS):
                            pe.matmul(s_bank(NBK)[g * PW:(g + 1) * PW, 0:TS], stationary(2 * g + odd), k_new[:, 2 * g + odd, :],
                                      start=(odd == 0), stop=False, skip_group_check=True)
                    for s in range(NT):
                        pe.wait_ge(k_in[s], b * 16 + 16)
                        for g in range(PAIRS):
                            mm = pe.matmul(s_bank(s // 2)[g * PW:(g + 1) * PW, :], stationary(2 * g + s % 2), k_ring[:, s, g, :],
                                           start=(s % 2 == 0), stop=False, skip_group_check=True)
                        mm.then_inc(sem["k_used"], 1)
                    if rel is None:
                        pe.wait_ge(sem["bias_in"], b * 16 + 16)
                    rows = c.head_rows[:].rearrange("k h i -> k (h i)") if rel is None else c.flip[:]
                    for j in range(NBK):
                        pe.matmul(s_bank(j)[:], rows, bias[:, j * 512:(j + 1) * 512], start=False, stop=True, skip_group_check=True)
                    mm = pe.matmul(s_bank(NBK)[:, 0:TS], rows, bias[:, past:L], start=False, stop=(rel is not None),
                                   skip_group_check=True)
                    if rel is None:
                        mm = pe.matmul(s_bank(NBK)[:, 0:TS], c.query_rows[:].rearrange("k h i -> k (h i)"),
                                       c.causal[0:TS, 0:TS], start=False, stop=True, skip_group_check=True)
                    mm.then_inc(sem["scores"], 1)
                    if not first:
                        pe.wait_ge(sem["prob_t"], b * (NBK + 1))
                    for h in range(H):
                        mm = pe.transpose(c.bank[3 + h // 4][0:TS, (h % 4) * HD:(h % 4 + 1) * HD], v_new[:, h, :], c.ident[:])
                    mm.then_inc(sem["v_turned"], 1)
                    if not first:
                        values(b - 1, b - 1)
                    pe.wait_ge(sem["prob"], b + 1)
                    pe.wait_ge(sem["v_rows"], b + 1)
                    for k in range(NK):
                        mm = pe.transpose(c.bank[3 + k // 4][:, (k % 4) * P:(k % 4 + 1) * P], prob[:, k * P:(k + 1) * P], c.ident[:])
                        if k % 4 == 3:
                            mm.then_inc(sem["turned"], 1)
                    pe.transpose(c.bank[5][0:TS, 0:P], prob[:, past:L], c.ident[:]).then_inc(sem["turned"], 1)
                    if not first:
                        turn_back(b - 1)

                def values(b, kept):
                    if not (isinstance(kept, int) and kept == 0):
                        pe.wait_ge(sem["y"], kept)
                        own_instruction(c, pe)
                    for n, k in enumerate([NK, *range(NK)]):
                        if k < NK and k % KV == 0:
                            pe.wait_ge(v_in[k // KV], b * 16 + 16)
                        for g in range(PAIRS):
                            pair, both = slice(g * PW, (g + 1) * PW), slice(2 * g * HD, 2 * (g + 1) * HD)
                            if k < NK:
                                lhs, rhs = prob_t[:, k, pair], v_ring[:, k // KV, k % KV, both]
                            else:
                                lhs, rhs = prob_t[0:TS, k, pair], v_rows[:, both]
                            mm = pe.matmul(c.bank[6][pair, 0:2 * HD], lhs, rhs, start=(n == 0), stop=(n == NK),
                                           skip_group_check=True)
                        if k == NK:
                            mm.then_inc(sem["v_rows_used"], 1)
                        elif k % KV == KV - 1:
                            mm.then_inc(sem["v_used"], 1)

                def turn_back(b):
                    pe.wait_ge(sem["o_rows"], b + 1)
                    for odd in range(2):
                        mm = pe.transpose(c.bank[7][:, odd * P:(odd + 1) * P], o_rows[:, odd * HD:(odd + 1) * HD], c.ident[:])
                    mm.then_inc(sem["o_turned"], 1)

                sequence(0, True)
                sequence(1, False)
                with pe.Fori(2, NB) as b:
                    sequence(b, False)
                pe.wait_ge(sem["prob_t"], NB * (NBK + 1))
                values(NB - 1, NB - 1)
                turn_back(NB - 1)

            @block.scalar
            def _(act):
                def sequence(b, first):
                    act.wait_ge(sem["maxed"], b + 1)
                    if not first:
                        act.wait_ge(sem["turned"], b * (NBK + 1))
                    act.activation(prob[:], c.scores[:, 0:L], ACT.Exp, bias=stat[:, 0:1],
                                   accum_out=stat[:, 1:2]).then_inc(sem["exped"], 1)
                    act.wait_ge(sem["v_turned"], b + 1)
                    if not first:
                        act.wait_ge(sem["v_rows_used"], b)
                    act.activation(v_rows[:, 0:512], c.bank[3][0:TS, :], ACT.Copy)
                    act.activation(v_rows[:, 512:1024], c.bank[4][0:TS, :], ACT.Copy).then_inc(sem["v_rows"], 1)
                    for j in range(NBK):
                        act.wait_ge(sem["turned"], b * (NBK + 1) + (j + 1))
                        act.activation(prob_t[:, 4 * j:4 * j + 4, :].rearrange("p k q -> p (k q)"), c.bank[3 + j][:],
                                       ACT.Copy).then_inc(sem["prob_t"], 1)
                    act.wait_ge(sem["turned"], b * (NBK + 1) + (NBK + 1))
                    act.activation(prob_t[0:TS, NK, :], c.bank[5][0:TS, 0:P], ACT.Copy).then_inc(sem["prob_t"], 1)

                first_then_loop(act, NB, sequence)

            @block.vector
            def _(dve):
                dve.wait_ge(sem["new_in"], 48)
                dve.wait_ge(sem["zeroed"], 1)

                def pick(b, first):
                    if not first:
                        dve.wait_ge(sem["v_turned"], b)
                    at = bass.ds(b * TS, TS)
                    dve.tensor_scalar(q_pad[:, :, 0:TS], new[:, 0, :, at], QK_SCALE, None, ALU.mult).then_inc(sem["picked"], 1)
                    dve.tensor_copy(k_new[:], new[:, 1, :, at]).then_inc(sem["picked"], 1)
                    dve.tensor_copy(v_new[:], new[:, 2, :, at]).then_inc(sem["picked"], 1)

                def softmax(b):
                    dve.wait_ge(sem["scores"], b + 1)
                    dve.tensor_reduce(stat[:, 0:1], c.scores[:, 0:L], AX.X, ALU.max, negate=True).then_inc(sem["maxed"], 1)
                    dve.wait_ge(sem["exped"], b + 1)
                    dve.reciprocal(stat[:, 2:3], stat[:, 1:2]).then_inc(sem["recip"], 1)
                    dve.wait_ge(sem["recip"], b + 1)
                    dve.tensor_scalar(prob[:], prob[:], stat[:, 2:3], None, ALU.mult).then_inc(sem["prob"], 1)

                def rows_of(b):
                    dve.wait_ge(sem["v_used"], b * NT + NT)
                    dve.tensor_copy(o_rows[:], c.bank[6][:, 0:2 * HD]).then_inc(sem["o_rows"], 1)

                def keep(b):
                    dve.wait_ge(sem["o_turned"], b + 1)
                    pairs_of = y[:, :, bass.ds(b * TS, TS)].rearrange("p (g r) i -> p g r i", r=2)
                    for odd in range(2):
                        turned = c.bank[7][:, odd * P:(odd + 1) * P].rearrange("p (g r i) -> p g r i", r=2, i=TS)
                        op = dve.tensor_copy(pairs_of[:, :, odd], turned[:, :, odd])
                    op.then_inc(sem["y"], 1)

                pick(0, True)
                softmax(0)
                pick(1, False)
                softmax(1)
                rows_of(0)
                with dve.Fori(2, NB) as b:
                    pick(b, False)
                    keep(b - 2)
                    softmax(b)
                    rows_of(b - 1)
                keep(NB - 2)
                rows_of(NB - 1)
                keep(NB - 1)


class Residual:

    def __init__(self, c, tmp, name, row):
        self.c, self.row = c, row
        self.sample = c.sb(f"{name}_sample", [P, NB, TS], F32, tmp)
        self.scaled, self.added = c.sem(f"{name}_scaled"), c.sem(f"{name}_added")

    def add(self, dve, n, m, out):
        c, gate = self.c, lambda lo, hi: self.c.ada[:, m + self.row * DC, lo:hi]
        tail = out[1][:, TP - HALF:HALF].rearrange("p (b i) -> p b i", i=TS)
        acc_tail = c.acc[:, m, TP:T].rearrange("p (b i) -> p b i", i=TS)
        dve.wait_ge(self.added, n + 2)
        dve.tensor_tensor(self.sample[:], tail, gate(1, NC9).unsqueeze(2).broadcast_to([P, NB, TS]),
                          ALU.mult).then_inc(self.scaled, 1)
        dve.scalar_tensor_tensor(out=c.acc[:, m, 0:HALF], in0=out[0], scalar=gate(0, 1),
                                 in1=c.acc[:, m, 0:HALF], op0=ALU.mult, op1=ALU.add)
        dve.scalar_tensor_tensor(out=c.acc[:, m, HALF:TP], in0=out[1][:, 0:TP - HALF], scalar=gate(0, 1),
                                 in1=c.acc[:, m, HALF:TP], op0=ALU.mult, op1=ALU.add)
        dve.wait_ge(self.scaled, n + 1)
        dve.tensor_tensor(acc_tail, acc_tail, self.sample[:], ALU.add).then_inc(self.added, 1)


def build_mix(c, tiles, yt, x_dram):
    nc = c.nc
    NMIX = 3 * DC
    with ExitStack() as tmp:
        ws = WeightStream(c, tmp, "mix")
        res = Residual(c, tmp, "out_res", 2)
        y_hi = c.sb("mix_y_hi", [P, H, T], F32R, tmp)
        y_lo = c.sb("mix_y_lo", [P, H, T], F32R, tmp)
        work = c.sb("mix_work", [P, 2, T], F32, tmp)
        y_in = [c.sem(f"mix_y_in{b}") for b in range(2)]
        hi, lo, gate, scaled, merged = (c.sem(f"mix_{n}") for n in ("y_hi", "y_lo", "gate", "scaled", "merged"))
        acc_hi, acc_lo, x_in = c.sem("merged_hi"), c.sem("merged_lo"), c.sem("out_x_in")
        with nc.Block() as block:
            @block.sync
            def _(sp):
                ws.load(sp, tiles, 2 * NMIX + 2 * DC)

            @block.gpsimd
            def _(pool):
                ws.divide(pool, 2 * NMIX + 2 * DC)

            @block.scalar
            def _(act):
                def split(r, h):
                    act.wait_ge(y_in[h % 2], 16 * (r * (H // 2) + h // 2 + 1))
                    act.activation(y_hi[:, h], work[:, h % 2], ACT.Copy).then_inc(hi, 1)

                act.sem_inc(merged, 2)
                for r in range(2):
                    if r == 1:
                        act.wait_ge(merged, DC + 2)
                    for h in range(H):
                        if h >= 2:
                            act.wait_ge(lo, r * H + h - 1)
                        act.dma_start(work[:, h % 2], yt[r, h]).then_inc(y_in[h % 2], 16)
                        if h >= 1:
                            split(r, h - 1)
                    split(r, H - 1)
                    act.wait_ge(lo, r * H + H)
                    with act.Fori(0, DC // 2) as i:
                        for b in range(2):
                            m = i * 2 + b
                            act.wait_ge(ws.used, m * 3 + (r * NMIX + 3 + SPLIT))
                            act.wait_ge(merged, m + (r * DC + 1))
                            for j in range(2):
                                act.activation(work[:, b, j * HALF:(j + 1) * HALF], c.halves(4 * b + 2)[j],
                                               ACT.Sigmoid).then_inc(gate, 1)
                for k in range(DC):
                    act.wait_ge(merged, DC + k + 3)
                    act.activation(c.act_hi[:, k], c.acc[:, k], ACT.Copy).then_inc(acc_hi, 1)
                act.wait_ge(acc_lo, DC)
                act.dma_start(c.acc[:], x_dram.rearrange("k p t -> p k t")).then_inc(x_in, 16)

            @block.tensor
            def _(pe):
                def merge(r):
                    def columns(i, first):
                        for b in range(2):
                            m = i * 2 + b
                            pe.wait_ge(merged, m + (r * DC + 1))
                            for j in range(3):
                                n, slot = m * 3 + (r * NMIX + j), (3 * b + j) % 2
                                if j == 2:
                                    ws.multiply(pe, n, slot, c.halves(4 * b), y_hi, y_lo, 0, True, True,
                                                chunk_ready=lo if first and b == 0 else None, ready_from=r * H)
                                else:
                                    ws.multiply(pe, n, slot, c.halves(4 * b + 2), c.act_hi, c.act_lo,
                                                j * KT, j == 0, j == 1)

                    first_then_loop(pe, DC // 2, columns)

                def output(i, first):
                    for b in range(2):
                        m = i * 2 + b
                        pe.wait_ge(res.added, m + 1)
                        for kh in range(2):
                            ws.multiply(pe, m * 2 + (2 * NMIX + kh), kh, c.halves(2 * b), c.act_hi, c.act_lo,
                                        kh * KT, kh == 0, kh == 1, chunk_ready=acc_lo if first and b == 0 else None)

                merge(0)
                merge(1)
                first_then_loop(pe, DC // 2, output)

            @block.vector
            def _(dve):
                dve.sem_inc(res.added, 2)
                for r in range(2):
                    for h in range(H):
                        dve.wait_ge(hi, r * H + h + 1)
                        dve.tensor_tensor(y_lo[:, h], work[:, h % 2], y_hi[:, h].bitcast(F32), ALU.subtract).then_inc(lo, 1)
                    with dve.Fori(0, DC // 2) as i:
                        for b in range(2):
                            m = i * 2 + b
                            dve.wait_ge(gate, m * 2 + (2 * r * DC + 2))
                            out = c.halves(4 * b)
                            for j in range(2):
                                at = slice(j * HALF, (j + 1) * HALF)
                                dst = c.acc[:, m, at] if r == 0 else work[:, b, at]
                                op = dve.tensor_tensor(dst, out[j], work[:, b, at], ALU.mult)
                            if r == 0:
                                op.then_inc(merged, 1)
                            else:
                                op.then_inc(scaled, 1)
                                dve.wait_ge(scaled, m + 1)
                                dve.tensor_tensor(c.acc[:, m], c.acc[:, m], work[:, b], ALU.add).then_inc(merged, 1)
                for k in range(DC):
                    dve.wait_ge(acc_hi, k + 1)
                    dve.tensor_tensor(c.act_lo[:, k], c.acc[:, k], c.act_hi[:, k].bitcast(F32),
                                      ALU.subtract).then_inc(acc_lo, 1)
                dve.wait_ge(x_in, 16)
                with dve.Fori(0, DC // 2) as i:
                    for b in range(2):
                        m = i * 2 + b
                        dve.wait_ge(ws.used, m * 2 + (2 * NMIX + 2 + SPLIT))
                        res.add(dve, m, m, c.halves(2 * b))


def build_retrieval(c, tiles, sub_keys, key1_t, key2_t, gate_t):
    nc = c.nc
    NHD = H // 2
    with ExitStack() as tmp:
        ws = WeightStream(c, tmp, "query")
        keys = c.sb("sub_keys_sb", [P, 2 * H, NKEY], F32, tmp)
        query = c.sb("query_sb", [P, 2, T], F32, tmp)
        score = c.sb("key_scores", [P, 2, TT, 2, NKEY], F32, tmp)
        rest = c.sb("scores_rest", [P, TT, 2, NKEY], F32, tmp)
        top = c.sb("top_keys", [P, TT, 2, TOPK], F32, tmp)
        top_at = c.sb("top_keys_at", [P, TT, 2, TOPK], U32, tmp)
        top_atf = c.sb("top_keys_atf", [P, TT, 2, TOPK], F32, tmp)
        cand = c.sb("candidates", [P, TT, TOPK, TOPK], F32, tmp)
        crest = rest[:].rearrange("p t c n -> p t (c n)")
        best = c.sb("best", [P, TT, TOPK], F32, tmp)
        best_at = c.sb("best_at", [P, TT, TOPK], U32, tmp)
        rank_at = cand[:].rearrange("p t a b -> p (t a b)")[:, 0:2 * TT * TOPK].bitcast(U32).rearrange(
            "p (s t k) -> p s t k", s=2, t=TT)
        rank = c.sb("rank", [P, 2, TT, TOPK], F32, tmp)
        shifted = c.sb("best_shifted", [P, TT, TOPK], F32, tmp)
        total = c.sb("gate_total", [P, 2, TT], F32, tmp)
        found = [out[:].rearrange("p (t k) -> p t k", k=H * TOPK) for out in (key1_t, key2_t, gate_t)]
        keys_in, query_ready = c.sem("sub_keys_in"), c.sem("query_ready")
        scored, score_ready, score_free = c.sem("scored"), c.sem("score_ready"), c.sem("score_free")
        step, expd, turned = c.sem("topk_step"), c.sem("gate_exp"), c.sem("found_turned")
        gate_ready = c.sem("gate_t_ready")
        STEPS = 21
        with nc.Block() as block:
            @block.sync
            def _(sp):
                sp.dma_start(keys[:], sub_keys).then_inc(keys_in, 16)
                ws.load(sp, tiles, 2 * DC)

            @block.gpsimd
            def _(pool):
                ws.divide(pool, 2 * DC)

            @block.tensor
            def _(pe):
                def score_of(m, b):
                    pe.wait_ge(query_ready, m * 2 + 2)
                    pe.wait_ge(score_ready, m + 1)
                    for t in range(TT):
                        mm = pe.matmul(c.bank[4 + t // 4][:, (t % 4) * P:(t % 4 + 1) * P],
                                       query[:, b, t * P:(t + 1) * P], keys[:, m, :], start=True, stop=True)
                    mm.then_inc(scored, 1)

                def columns(i, first):
                    for b in range(2):
                        m = i * 2 + b
                        if not first:
                            pe.wait_ge(query_ready, m * 2 - 2)
                        for kh in range(2):
                            ws.multiply(pe, m * 2 + kh, kh, c.halves(2 * b), c.act_hi, c.act_lo, kh * KT, kh == 0, kh == 1)
                        if not (first and b == 0):
                            score_of(m - 1, 1 - b)

                pe.wait_ge(keys_in, 16)
                first_then_loop(pe, DC // 2, columns)
                score_of(DC - 1, 1)
                pe.wait_ge(step, H * STEPS)
                for j in range(3):
                    for t in range(TT):
                        mm = pe.transpose(c.bank[2 * j + t // 4][:, (t % 4) * P:(t % 4 + 1) * P], found[j][:, t, :], c.ident[:])
                    mm.then_inc(turned, 1)

            @block.scalar
            def _(act):
                def evacuate(m, b, first):
                    act.wait_ge(ws.used, m * 2 + (2 + SPLIT))
                    if not first:
                        act.wait_ge(scored, m - 1)
                    for j in range(2):
                        act.activation(query[:, b, j * HALF:(j + 1) * HALF], c.halves(2 * b)[j],
                                       ACT.Copy).then_inc(query_ready, 1)

                def keep(m, hb, side):
                    act.wait_ge(scored, m + 1)
                    act.activation(score[:, hb, 0:4, side, :], c.bank[4][:].rearrange("p (t n) -> p t n", n=NKEY), ACT.Copy)
                    act.activation(score[:, hb, 4, side, :], c.bank[5][:, 0:NKEY], ACT.Copy).then_inc(score_ready, 1)

                def head_exp(h):
                    act.wait_ge(step, h * STEPS + 10)
                    act.activation(shifted[:], shifted[:], ACT.Exp).then_inc(expd, 1)

                def two_heads(i, first):
                    for hb in range(2):
                        h = i * 2 + hb
                        for side in range(2):
                            m = h * 2 + side
                            evacuate(m, side, first and hb == 0)
                            if side == 1:
                                act.wait_ge(score_free, h + 1)
                                keep(m - 1, hb, 0)
                            elif not (first and hb == 0):
                                keep(m - 1, 1 - hb, 1)
                                if not (first and hb == 1):
                                    head_exp(h - 2)

                act.sem_inc(score_ready, 1)
                first_then_loop(act, NHD, two_heads)
                keep(DC - 1, 1, 1)
                head_exp(H - 2)
                head_exp(H - 1)

            @block.vector
            def _(dve):
                dve.sem_inc(score_free, 2)

                def retrieve(i, first):
                    for hb in range(2):
                        head(i * 2 + hb, hb)

                def head(h, hb):
                    def done(k, searches=False):
                        dve.wait_ge(step, h * STEPS + k)
                        if searches:
                            own_instruction(c, dve)

                    pairs = [(t, s) for t in range(TT) for s in range(2)]
                    dve.wait_ge(score_ready, h * 2 + 3)
                    own_instruction(c, dve)
                    for t, s in pairs:
                        op = dve.max(top[:, t, s, 0:8], score[:, hb, t, s, :])
                    op.then_inc(step, 1)
                    done(1, searches=True)
                    for t, s in pairs:
                        dve.max_index(top_at[:, t, s, 0:8], top[:, t, s, 0:8], score[:, hb, t, s, :])
                        op = dve.match_replace(rest[:, t, s, :], top[:, t, s, 0:8], score[:, hb, t, s, :], LOWEST)
                    op.then_inc(step, 1)
                    done(2, searches=True)
                    for t, s in pairs:
                        op = dve.max(top[:, t, s, 8:16], rest[:, t, s, :])
                    op.then_inc(step, 1)
                    done(3, searches=True)
                    dve.sem_inc(score_free, 1)
                    for t, s in pairs:
                        op = dve.max_index(top_at[:, t, s, 8:16], top[:, t, s, 8:16], rest[:, t, s, :])
                    op.then_inc(step, 1)
                    done(4)
                    dve.tensor_copy(top_atf[:], top_at[:])
                    dve.tensor_tensor(cand[:], top[:, :, 0, :].unsqueeze(3).broadcast_to([P, TT, TOPK, TOPK]),
                                      top[:, :, 1, :].unsqueeze(2).broadcast_to([P, TT, TOPK, TOPK]),
                                      ALU.add).then_inc(step, 1)
                    done(5, searches=True)
                    flat = cand[:].rearrange("p t a b -> p t (a b)")
                    for t in range(TT):
                        op = dve.max(best[:, t, 0:8], flat[:, t, :])
                    op.then_inc(step, 1)
                    done(6, searches=True)
                    for t in range(TT):
                        dve.max_index(best_at[:, t, 0:8], best[:, t, 0:8], flat[:, t, :])
                        op = dve.match_replace(crest[:, t, :], best[:, t, 0:8], flat[:, t, :], LOWEST)
                    op.then_inc(step, 1)
                    done(7, searches=True)
                    for t in range(TT):
                        op = dve.max(best[:, t, 8:16], crest[:, t, :])
                    op.then_inc(step, 1)
                    done(8, searches=True)
                    for t in range(TT):
                        op = dve.max_index(best_at[:, t, 8:16], best[:, t, 8:16], crest[:, t, :])
                    op.then_inc(step, 1)
                    done(9)
                    dve.tensor_tensor(shifted[:], best[:], best[:, :, 0:1].broadcast_to([P, TT, TOPK]),
                                      ALU.subtract).then_inc(step, 1)
                    dve.tensor_scalar(rank_at[:, 0], best_at[:], 4, None, ALU.logical_shift_right)
                    dve.tensor_scalar(rank_at[:, 1], best_at[:], TOPK - 1, None, ALU.bitwise_and).then_inc(step, 1)
                    done(11)
                    dve.tensor_copy(rank[:], rank_at).then_inc(step, 1)
                    done(12)
                    for s in range(2):
                        dve.tensor_tensor(cand[:], c.iota[:, 0:TOPK].unsqueeze(1).unsqueeze(1).broadcast_to([P, TT, TOPK, TOPK]),
                                          rank[:, s].unsqueeze(3).broadcast_to([P, TT, TOPK, TOPK]),
                                          ALU.is_equal).then_inc(step, 1)
                        done(13 + 3 * s)
                        dve.tensor_tensor(cand[:], cand[:], top_atf[:, :, s, :].unsqueeze(2).broadcast_to([P, TT, TOPK, TOPK]),
                                          ALU.mult).then_inc(step, 1)
                        done(14 + 3 * s)
                        dve.tensor_reduce(found[s][:, :, bass.ds(h * TOPK, TOPK)], cand[:], AX.X, ALU.add).then_inc(step, 1)
                        done(15 + 3 * s)
                    dve.wait_ge(expd, h + 1)
                    dve.tensor_reduce(total[:, 0], shifted[:], AX.X, ALU.add).then_inc(step, 1)
                    done(19)
                    dve.reciprocal(total[:, 1], total[:, 0]).then_inc(step, 1)
                    done(20)
                    dve.tensor_tensor(found[2][:, :, bass.ds(h * TOPK, TOPK)], shifted[:],
                                      total[:, 1].unsqueeze(2).broadcast_to([P, TT, TOPK]), ALU.mult).then_inc(step, 1)
                    done(21)

                first_then_loop(dve, NHD, retrieve)
                for j, out in enumerate((key1_t, key2_t, gate_t)):
                    dve.wait_ge(turned, j + 1)
                    dve.tensor_copy(out[:, 0:512], c.bank[2 * j][:])
                    op = dve.tensor_copy(out[:, 512:T], c.bank[2 * j + 1][:, 0:T - 512])
                op.then_inc(gate_ready, 1)
                dve.wait_ge(gate_ready, 1)


def build_gates(c, key1_t, key2_t, gate_t, gates):
    nc = c.nc
    Q = 4
    NQ = GB // Q
    SLOTS = 4
    AHEAD = 2
    with ExitStack() as tmp:
        gate_hi, gate_lo = (c.sb(f"gate_{n}", [P, T], F32R, tmp) for n in ("hi", "lo"))
        rounded = c.sem("gates_rounded")
        gbuf = c.sb("gate_batch", [P, 2, NKEY, GB], F32, tmp)
        second = [c.sb(f"onehot_second{s}", [P, Q, NKEY], F32, tmp) for s in range(SLOTS)]
        kind = [F32R if s % 2 == 0 else F32 for s in range(SLOTS)]
        onehot = [c.sb(f"onehot{s}", [P, Q, NKEY], kind[s], tmp) for s in range(SLOTS)]
        wide = [c.sb(f"gated{s}", [P, Q, NKEY], kind[s], tmp) for s in range(SLOTS)]
        wide_lo = {s: c.sb(f"gated_lo{s}", [P, Q, NKEY], F32R, tmp) for s in range(0, SLOTS, 2)}
        sel, gated, low, both, product, kept = (
            c.sem(f"gates_{n}") for n in ("sel", "gated", "low", "both", "product", "kept"))
        stored = [c.sem(f"gates_stored{b}") for b in range(2)]

        def of(v, n):
            return v[:, bass.ds(n * Q, Q)].unsqueeze(2).broadcast_to([P, Q, NKEY])

        with nc.Block() as block:
            @block.gpsimd
            def _(pool):
                with pool.Fori(0, T // Q // SLOTS) as i:
                    for s in range(SLOTS):
                        n = i * SLOTS + s
                        pool.wait_ge(sel, n + 1)
                        gate = gate_hi[:].bitcast(F32) if kind[s] == F32R else gate_t[:]
                        pool.tensor_tensor(wide[s][:], second[s][:], of(gate, n), ALU.mult).then_inc(gated, 1)

            @block.vector
            def _(dve):
                dve.tensor_copy(gate_hi[:], gate_t[:]).then_inc(rounded, 1)
                dve.wait_ge(rounded, 1)
                dve.tensor_tensor(gate_lo[:], gate_t[:], gate_hi[:].bitcast(F32), ALU.subtract).then_inc(rounded, 1)
                dve.wait_ge(rounded, 2)
                dve.sem_inc(product, SLOTS)
                every = c.iota[:].unsqueeze(1).broadcast_to([P, Q, NKEY])
                with dve.Fori(0, T // Q // SLOTS) as i:
                    for s in range(SLOTS):
                        n = i * SLOTS + s
                        dve.wait_ge(product, n + 1)
                        dve.tensor_tensor(second[s][:], every, of(key2_t, n), ALU.is_equal).then_inc(sel, 1)
                        dve.tensor_tensor(onehot[s][:], every, of(key1_t, n), ALU.is_equal).then_inc(both, 1)

            @block.tensor
            def _(pe):
                with pe.Fori(0, T // Q // SLOTS) as i:
                    for s in range(SLOTS):
                        n = i * SLOTS + s
                        pe.wait_ge(both, n + 1)
                        pe.wait_ge(gated, n + 1)
                        if s in wide_lo:
                            pe.wait_ge(low, i * (SLOTS // 2) + (s // 2 + 1))
                        pe.wait_ge(kept, n + 1)
                        for j in range(Q):
                            out = c.bank[s][:, j * NKEY:(j + 1) * NKEY]
                            mm = pe.matmul(out, onehot[s][:, j, :], wide[s][:, j, :], start=True, stop=(s not in wide_lo))
                            if s in wide_lo:
                                mm = pe.matmul(out, onehot[s][:, j, :], wide_lo[s][:, j, :], start=False, stop=True)
                        mm.then_inc(product, 1)

            @block.scalar
            def _(act):
                def make_low(n, s):
                    if s not in wide_lo:
                        return
                    act.wait_ge(sel, n + 1)
                    for j in range(Q):
                        op = act.activation(wide_lo[s][:, j, :], second[s][:, j, :], ACT.Copy,
                                            scale=gate_lo[:, bass.ds(n * Q + j, 1)].bitcast(F32))
                    op.then_inc(low, 1)

                def keep(b, q, n, s):
                    act.wait_ge(product, n + (1 + SLOTS))
                    act.activation(gbuf[:, b, :, bass.ds(q * Q, Q)].rearrange("p c t -> p t c"),
                                   c.bank[s][:].rearrange("p (t c) -> p t c", c=NKEY), ACT.Copy).then_inc(kept, 1)

                def batch(i, b, last):
                    whole = NQ // SLOTS - (1 if last else 0)
                    with act.Fori(0, whole) as r:
                        for s in range(SLOTS):
                            n = (i * 2 + b) * NQ + (r * SLOTS + s)
                            make_low(n + AHEAD, (s + AHEAD) % SLOTS)
                            keep(b, r * SLOTS + s, n, s)
                    if last:
                        for q in range(whole * SLOTS, NQ):
                            n = (i * 2 + b) * NQ + q
                            if q < NQ - AHEAD:
                                make_low(n + AHEAD, (q + AHEAD) % SLOTS)
                            keep(b, q, n, q % SLOTS)

                def batches(i, first, last=False):
                    for b in range(2):
                        if not first:
                            act.wait_ge(stored[b], i * 16)
                        batch(i, b, last and b == 1)

                act.sem_inc(kept, SLOTS)
                for n in range(AHEAD):
                    make_low(n, n)
                batches(0, True)
                with act.Fori(1, NGB // 2 - 1) as i:
                    batches(i, False)
                batches(NGB // 2 - 1, False, last=True)

            @block.sync
            def _(sp):
                with sp.Fori(0, NGB // 2) as i:
                    for b in range(2):
                        sp.wait_ge(kept, (i * 2 + b) * NQ + (NQ + SLOTS))
                        sp.dma_start(gates[i * 2 + b], gbuf[:, b]).then_inc(stored[b], 16)
                for b in range(2):
                    sp.wait_ge(stored[b], 16 * (NGB // 2))


def build_experts(c, tiles, gates):
    nc = c.nc
    NU = 2 * GROUP
    NV = DC
    with ExitStack() as tmp:
        ws = WeightStream(c, tmp, "expert")
        res = Residual(c, tmp, "expert_res", 5)
        w_hi = c.sb("gated_act_hi", [P, GROUP, T], F32R, tmp)
        w_lo = c.sb("gated_act_lo", [P, GROUP, T], F32R, tmp)
        gate = c.sb("gate_chunk", [P, 2, T], F32, tmp)
        hidden = c.sb("hidden", [P, T], F32, tmp)
        gate_in = [c.sem(f"expert_gate_in{b}") for b in range(2)]
        gelu, gated, hi, lo = (c.sem(f"expert_{n}") for n in ("gelu", "gated", "hi", "lo"))
        with nc.Block() as block:
            @block.sync
            def _(sp):
                with sp.Fori(0, NGROUP) as g:
                    with sp.Fori(0, NU // RAW) as i:
                        ws.load_four(sp, tiles, g * (NU + NV) + i * RAW)
                    with sp.Fori(0, NV // RAW) as i:
                        ws.load_four(sp, tiles, g * (NU + NV) + (i * RAW + NU))

            @block.gpsimd
            def _(pool):
                ws.divide(pool, NGROUP * (NU + NV))

            @block.tensor
            def _(pe):
                with pe.Fori(0, NGROUP) as g:
                    with pe.Fori(0, GROUP // 2) as i:
                        for b in range(2):
                            j = i * 2 + b
                            pe.wait_ge(gelu, (g * GROUP + j) * 2 + 2)
                            for kh in range(2):
                                ws.multiply(pe, g * (NU + NV) + j * 2 + kh, kh, c.halves(2 * b), c.act_hi, c.act_lo,
                                            kh * KT, kh == 0, kh == 1)

                    def sums(i, first):
                        for b in range(2):
                            m = i * 2 + b
                            pe.wait_ge(res.added, g * NV + m + 1)
                            ws.multiply(pe, g * (NU + NV) + (m + NU), b, c.halves(4 + 2 * b), w_hi, w_lo, 0, True, True,
                                        chunk_ready=lo if first and b == 0 else None,
                                        ready_from=g * GROUP + 1)

                    first_then_loop(pe, NV // 2, sums)

            @block.scalar
            def _(act):
                act.sem_inc(gelu, 4)
                with act.Fori(0, NGROUP) as g:
                    with act.Fori(0, GROUP // 2) as i:
                        for b in range(2):
                            j = i * 2 + b
                            n = g * GROUP + j
                            act.wait_ge(gated, n + 1)
                            act.dma_start(gate[:, b].rearrange("p (q t) -> p q t", t=GB),
                                          gates[:, :, n, :].rearrange("q p t -> p q t")).then_inc(gate_in[b], 16)
                            act.wait_ge(ws.used, g * (NU + NV) + j * 2 + (2 + SPLIT))
                            act.wait_ge(lo, n + 1)
                            for h in range(2):
                                act.activation(hidden[:, h * HALF:(h + 1) * HALF], c.halves(2 * b)[h],
                                               ACT.Gelu).then_inc(gelu, 1)
                            act.wait_ge(gated, n + 3)
                            act.activation(w_hi[:, j], hidden[:], ACT.Copy).then_inc(hi, 1)

            @block.vector
            def _(dve):
                dve.sem_inc(gated, 2)
                dve.sem_inc(lo, 1)
                dve.sem_inc(res.added, 2)
                with dve.Fori(0, NGROUP) as g:
                    with dve.Fori(0, GROUP // 2) as i:
                        for b in range(2):
                            j = i * 2 + b
                            n = g * GROUP + j
                            dve.wait_ge(gelu, n * 2 + (2 + 4))
                            dve.wait_ge(gate_in[b], (g * (GROUP // 2) + i) * 16 + 16)
                            dve.tensor_tensor(hidden[:], hidden[:], gate[:, b], ALU.mult).then_inc(gated, 1)
                            dve.wait_ge(hi, n + 1)
                            dve.tensor_tensor(w_lo[:, j], hidden[:], w_hi[:, j].bitcast(F32), ALU.subtract).then_inc(lo, 1)
                    with dve.Fori(0, NV // 2) as i:
                        for b in range(2):
                            m = i * 2 + b
                            dve.wait_ge(ws.used, g * (NU + NV) + m + (NU + 1 + SPLIT))
                            res.add(dve, g * NV + m, m, c.halves(4 + 2 * b))


def tiles_of(w):
    d, m = w.shape
    kh = d // (KT * P)
    return np.ascontiguousarray(w.reshape(kh, KT, P, m // P, P).transpose(3, 0, 2, 1, 4)).reshape(
        m // P * kh, P, KT * P)


def lay_out(a):
    feature_major = lambda v: np.ascontiguousarray(v.reshape(-1, P).T)
    chunked = lambda v: np.ascontiguousarray(v.T.reshape(DC, P, -1))
    x = np.concatenate([a["x_prompt"][0], a["x_sample"].reshape(NB * TS, D)])
    cond = np.concatenate([a["c_prompt"], a["c_sample"]])
    w_in = a["w_in"][0]
    f0, f1 = 3 * H * HD, 3 * H * HD + H
    g0 = f1 + 3 * H * HD
    gates = [tiles_of(w_in[:, g0 + r * D:g0 + (r + 1) * D]).reshape(DC, 2, P, KT * P) for r in range(2)]
    branches = [tiles_of(a[n][0]).reshape(DC, 1, P, KT * P) for n in ("w_branch_fox", "w_branch_band")]
    return {
        "x": chunked(x),
        "cond": np.pad(cond.T.reshape(DC, P, NC9).transpose(1, 0, 2), ((0, 0), (0, 0), (0, QUAD - NC9))),
        "w_ada": np.ascontiguousarray(a["w_ada"][0].reshape(RAW, DC // RAW, P, 6 * D // 512, 512).transpose(
            3, 0, 2, 1, 4)).reshape(6 * D // 512 * RAW, P, DC // RAW, 512),
        "b_ada": feature_major(a["b_ada"][0]),
        "norm_mix": feature_major(a["norm_mix"][0]),
        "norm_ffn": feature_major(a["norm_ffn"][0]),
        "norm_final": feature_major(a["norm_final"]),
        "w_heads": tiles_of(np.concatenate([np.pad(w_in[:, f0:f1], ((0, 0), (0, P - H))), w_in[:, :f0], w_in[:, f1:g0]],
                                           axis=1)),
        "cache_logf": np.ascontiguousarray(a["cache_fox_logf"][0].reshape(NB, PAST // P, P, H).transpose(
            2, 1, 0, 3)).reshape(P, PAST // P, NB * H),
        "fox_k": np.ascontiguousarray(a["cache_fox_k"][0].reshape(NB, 2, 512, 4, 2, HD).transpose(
            0, 1, 4, 5, 3, 2)).reshape(NB * 4, P, 2048),
        "fox_v": np.ascontiguousarray(a["cache_fox_v"][0].reshape(NB, 4, 2, P, H * HD).transpose(
            0, 1, 3, 2, 4)).reshape(NB * 4, P, 2048),
        "band_k": np.ascontiguousarray(a["cache_band_k"][0].reshape(NB, BW, 4, 2, HD).transpose(
            0, 3, 4, 2, 1)).reshape(NB * 2, P, 2048),
        "band_v": np.ascontiguousarray(a["cache_band_v"][0].reshape(NB, 2, 2, P, H * HD).transpose(
            0, 1, 3, 2, 4)).reshape(NB * 2, P, 2048),
        "rel": np.pad(a["rel_bias"][0][:, ::-1], ((0, 0), (RPAD, 0)), mode="edge"),
        "b_forget": np.ascontiguousarray(np.broadcast_to(a["b_forget"][0], (P, H))),
        "w_mix": np.concatenate(
            [np.concatenate([gates[r], branches[r]], axis=1).reshape(DC * 3, P, KT * P) for r in range(2)]
            + [tiles_of(a["w_out"][0])]),
        "w_query": tiles_of(a["w_query"][0]),
        "sub_keys": np.ascontiguousarray(a["sub_keys"][0].reshape(2 * H, NKEY, P).transpose(2, 0, 1)),
        "experts": np.concatenate([
            a["expert_u"][0].reshape(P, NGROUP, GROUP, 2, KT, P).transpose(1, 2, 3, 5, 4, 0).reshape(
                NGROUP, 2 * GROUP, P, KT * P),
            a["expert_v"][0].reshape(P, NGROUP, GROUP, DC, P).transpose(1, 3, 0, 2, 4).reshape(
                NGROUP, DC, P, KT * P)], axis=1).reshape(-1, P, KT * P),
    }


def build(nc, inp, proj, logf, y_out):
    negf_p = nc.dram_tensor("negf_prompt", [H, TP], F32, kind="Internal").ap()
    negf_s = nc.dram_tensor("negf_sample", [NB * H, PAST + TS], F32, kind="Internal").ap()
    yt = nc.dram_tensor("mixer_out", [2, H, P, T], F32, kind="Internal").ap()
    gates = nc.dram_tensor("gate_matrix", [NGB, P, NKEY, GB], F32, kind="Internal").ap()
    with ExitStack() as ctx:
        c = Chip(nc, ctx)
        build_constants(c)
        c.end_phase()
        with ExitStack() as tmp:
            ada_small = (c.sb("cond_act", [P, DC, QUAD], F32, tmp), c.sb("ada_bias", [P, 6 * DC], F32, tmp),
                         c.sb("ada_add_up", [P, NC9], F32, tmp))
            build_ada(c, ada_small, inp["w_ada"], inp["b_ada"], inp["cond"])
            c.end_phase()
            build_norm(c, "norm_mix", inp["x"], inp["norm_mix"], 1, 0)
            c.end_phase()
            build_projection(c, inp["w_heads"], inp["b_forget"], proj, logf, ada_small, inp["w_ada"])
            c.end_phase()
        build_forget_sums(c, logf, inp["cache_logf"], negf_p, negf_s)
        c.end_phase()
        build_prompt_attention(c, "fox_prompt", proj, 0, yt[0], negf_p=negf_p)
        c.end_phase()
        build_prompt_attention(c, "band_prompt", proj, 3 * H, yt[1], rel=inp["rel"])
        c.end_phase()
        build_sample_attention(c, "fox_sample", proj, 0, yt[0], PAST, inp["fox_k"], inp["fox_v"],
                               negf_s=negf_s.rearrange("(b h) t -> b h t", h=H))
        c.end_phase()
        build_sample_attention(c, "band_sample", proj, 3 * H, yt[1], BW, inp["band_k"], inp["band_v"], rel=inp["rel"])
        c.end_phase()
        build_mix(c, inp["w_mix"], yt, inp["x"])
        c.end_phase()
        build_norm(c, "norm_ffn", None, inp["norm_ffn"], 4, 3)
        c.end_phase()
        with ExitStack() as found:
            key1_t, key2_t = (c.sb(f"key{i}_t", [P, T], F32, found) for i in (1, 2))
            gate_t = c.sb("gate_t", [P, T], F32, found)
            build_retrieval(c, inp["w_query"], inp["sub_keys"], key1_t, key2_t, gate_t)
            c.end_phase()
            build_gates(c, key1_t, key2_t, gate_t, gates)
            c.end_phase()
        build_experts(c, inp["experts"], gates)
        c.end_phase()
        build_norm(c, "norm_final", None, inp["norm_final"], None, None, out_dram=y_out)
        c.end_phase(last=True)


def kernel(**inputs):
    import concourse.bacc as bacc
    from concourse.bass_utils import run_bass_kernel_spmd

    arrays = {f"in_{n}": v for n, v in lay_out({n: np.asarray(v) for n, v in inputs.items()}).items()}
    nc = bacc.Bacc("TRN2", target_bir_lowering=False, num_devices=1)
    inp = {n[3:]: nc.dram_tensor(n, v.shape, mybir.dt.from_np(v.dtype), kind="ExternalInput").ap()
           for n, v in arrays.items()}
    proj = nc.dram_tensor("out_proj", [6 * H, P, T], F32, kind="ExternalOutput").ap()
    logf = nc.dram_tensor("out_logf", [T, H], F32, kind="ExternalOutput").ap()
    y_out = nc.dram_tensor("out_y", [DC, P, T], F32, kind="ExternalOutput").ap()
    build(nc, inp, proj, logf, y_out)
    got = run_bass_kernel_spmd(nc, [arrays], core_ids=[0]).results[0]
    y = got["out_y"].reshape(D, T).T
    tokens = lambda j: got["out_proj"][j * H:(j + 1) * H].transpose(2, 0, 1)
    prompt = lambda j: np.ascontiguousarray(tokens(j)[None, None, :TP])
    sample = lambda j: np.ascontiguousarray(tokens(j)[TP:].reshape(1, NB, TS, H, HD))
    lf = got["out_logf"]
    return (np.ascontiguousarray(y[None, :TP]), np.ascontiguousarray(y[TP:]).reshape(NB, TS, D),
            prompt(1), prompt(2), np.ascontiguousarray(lf[None, None, :TP]), prompt(4), prompt(5),
            sample(1), sample(2), np.ascontiguousarray(lf[TP:]).reshape(1, NB, TS, H), sample(4), sample(5))
```
